# Optimizing a Trainium2 kernel written in Bass

```python
import jax, jax.numpy as jnp
from jax import lax
import numpy as np

D_MODEL = 2048
BATCH = 1
SEQ = 256
DEPTH = 1

N_MIXERS = 4
HEAD_DIM = 128
N_HEADS = D_MODEL // HEAD_DIM
Q_BLOCK = 128
EPS = 1e-6

FOX_FGATE_BIAS = 2.0

MLA_Q_RANK = 512
MLA_KV_RANK = 512
MLA_NOPE = 128
MLA_ROPE = 64
MLA_V = 128
ROPE_THETA = 10000.0

SGU_CHUNK = 128
SGU_WIDTH = D_MODEL
SGU_GROUP_DIM = 128
SGU_GROUPS = SGU_WIDTH // SGU_GROUP_DIM

D_FF = 5632
CONV_WIDTH = 3


def _n_layers_of(m):
    return len(range(m, DEPTH, N_MIXERS))

def rms_norm(x, gain):
    x32 = x.astype(jnp.float32)
    y = x32 * lax.rsqrt(jnp.mean(x32 * x32, axis=-1, keepdims=True) + EPS)
    return (y * gain.astype(jnp.float32)).astype(x.dtype)

def _sweep_query_blocks(block_fn, seq):
    out = lax.map(block_fn, jnp.arange(seq // Q_BLOCK))
    nb, b, qb, h, dv = out.shape
    return out.transpose(1, 0, 2, 3, 4).reshape(b, seq, h * dv)

def _causal_softmax(s, start, v):
    seq = s.shape[-1]
    q_pos = start + jnp.arange(Q_BLOCK)
    allowed = jnp.arange(seq)[None, :] <= q_pos[:, None]
    p = jax.nn.softmax(jnp.where(allowed, s, -jnp.inf), axis=-1)
    return jnp.einsum('bhqs,bshd->bqhd', p.astype(v.dtype), v)

def fox_mixer(h, w_in, b_f, q_gain, k_gain, w_out):
    bsz, seq, _ = h.shape
    hd = N_HEADS * HEAD_DIM
    q, k, v, f_logit = jnp.split(h @ w_in, [hd, 2 * hd, 3 * hd], axis=-1)
    q = rms_norm(q.reshape(bsz, seq, N_HEADS, HEAD_DIM), q_gain)
    k = rms_norm(k.reshape(bsz, seq, N_HEADS, HEAD_DIM), k_gain)
    v = v.reshape(bsz, seq, N_HEADS, HEAD_DIM)
    log_f = jax.nn.log_sigmoid(f_logit.astype(jnp.float32) + b_f.astype(jnp.float32))
    cum = jnp.cumsum(log_f, axis=1).transpose(0, 2, 1)
    scale = HEAD_DIM ** -0.5

    def block(i):
        start = i * Q_BLOCK
        qb = lax.dynamic_slice_in_dim(q, start, Q_BLOCK, axis=1)
        cq = lax.dynamic_slice_in_dim(cum, start, Q_BLOCK, axis=2)
        s = jnp.einsum('bqhd,bshd->bhqs', qb, k, preferred_element_type=jnp.float32) * scale
        s = s + (cq[..., :, None] - cum[:, :, None, :])
        return _causal_softmax(s, start, v)

    return _sweep_query_blocks(block, seq) @ w_out

def _rope_tables(positions):
    inv_freq = ROPE_THETA ** (-jnp.arange(0, MLA_ROPE, 2, dtype=jnp.float32) / MLA_ROPE)
    ang = positions.astype(jnp.float32)[..., None] * inv_freq
    return jnp.cos(ang)[:, :, None, :], jnp.sin(ang)[:, :, None, :]

def _apply_rope(x, cos, sin):
    x1, x2 = jnp.split(x.astype(jnp.float32), 2, axis=-1)
    return jnp.concatenate([x1 * cos - x2 * sin, x1 * sin + x2 * cos], axis=-1).astype(x.dtype)

def mla_mixer(h, positions, w_in, q_a_gain, kv_a_gain, w_q_b, w_kv_b, q_gain, k_gain, w_out):
    bsz, seq, _ = h.shape
    c_q, c_kv, k_rope = jnp.split(h @ w_in, [MLA_Q_RANK, MLA_Q_RANK + MLA_KV_RANK], axis=-1)
    q = (rms_norm(c_q, q_a_gain) @ w_q_b).reshape(bsz, seq, N_HEADS, MLA_NOPE + MLA_ROPE)
    kv = (rms_norm(c_kv, kv_a_gain) @ w_kv_b).reshape(bsz, seq, N_HEADS, MLA_NOPE + MLA_V)
    q_nope, q_rope = jnp.split(q, [MLA_NOPE], axis=-1)
    k_nope, v = jnp.split(kv, [MLA_NOPE], axis=-1)
    cos, sin = _rope_tables(positions)
    q_nope = rms_norm(q_nope, q_gain[:MLA_NOPE])
    k_nope = rms_norm(k_nope, k_gain[:MLA_NOPE])
    q_rope = _apply_rope(rms_norm(q_rope, q_gain[MLA_NOPE:]), cos, sin)
    k_rope = _apply_rope(rms_norm(k_rope[:, :, None, :], k_gain[MLA_NOPE:]), cos, sin)
    q = jnp.concatenate([q_nope, q_rope], axis=-1)
    k = jnp.concatenate([k_nope, jnp.broadcast_to(k_rope, (bsz, seq, N_HEADS, MLA_ROPE))], axis=-1)
    scale = (MLA_NOPE + MLA_ROPE) ** -0.5

    def block(i):
        start = i * Q_BLOCK
        qb = lax.dynamic_slice_in_dim(q, start, Q_BLOCK, axis=1)
        s = jnp.einsum('bqhd,bshd->bhqs', qb, k, preferred_element_type=jnp.float32) * scale
        return _causal_softmax(s, start, v)

    return _sweep_query_blocks(block, seq) @ w_out

def stick_breaking_mixer(h, w_in, q_gain, k_gain, w_out):
    bsz, seq, _ = h.shape
    hd = N_HEADS * HEAD_DIM
    q, k, v = jnp.split(h @ w_in, [hd, 2 * hd], axis=-1)
    q = rms_norm(q.reshape(bsz, seq, N_HEADS, HEAD_DIM), q_gain)
    k = rms_norm(k.reshape(bsz, seq, N_HEADS, HEAD_DIM), k_gain)
    v = v.reshape(bsz, seq, N_HEADS, HEAD_DIM)
    scale = HEAD_DIM ** -0.5

    def block(i):
        start = i * Q_BLOCK
        qb = lax.dynamic_slice_in_dim(q, start, Q_BLOCK, axis=1)
        z = jnp.einsum('bqhd,bshd->bhqs', qb, k, preferred_element_type=jnp.float32) * scale
        q_pos = start + jnp.arange(Q_BLOCK)
        strict = jnp.arange(seq)[None, :] < q_pos[:, None]
        log_keep = jnp.where(strict, -jax.nn.softplus(z), 0.0)
        after = lax.cumsum(log_keep, axis=3, reverse=True) - log_keep
        a = jnp.where(strict, jnp.exp(jax.nn.log_sigmoid(z) + after), 0.0)
        return jnp.einsum('bhqs,bshd->bqhd', a.astype(v.dtype), v)

    return _sweep_query_blocks(block, seq) @ w_out

def sgu_mixer(h, w_in, v_gain, w_s, b_s, w_out):
    bsz, seq, _ = h.shape
    u, vv = jnp.split(jax.nn.gelu(h @ w_in), 2, axis=-1)
    vv = rms_norm(vv, v_gain)
    n_chunks = seq // SGU_CHUNK
    vv = vv.reshape(bsz, n_chunks, SGU_CHUNK, SGU_GROUPS, SGU_GROUP_DIM)
    causal = jnp.tril(jnp.ones((SGU_CHUNK, SGU_CHUNK), dtype=bool))
    ws = jnp.where(causal[None], w_s, 0.0).astype(vv.dtype)
    mixed = jnp.einsum('gts,bnsgc->bntgc', ws, vv) + b_s.T[:, :, None]
    return (u * mixed.reshape(bsz, seq, SGU_WIDTH)) @ w_out

def conv_ffn(h, w_up, conv_w, conv_b, w_down):
    seq = h.shape[1]
    up = h @ w_up
    padded = jnp.pad(up, ((0, 0), (CONV_WIDTH - 1, 0), (0, 0)))
    y = conv_b + conv_w[0] * padded[:, 0:seq]
    for tap in range(1, CONV_WIDTH):
        y = y + conv_w[tap] * padded[:, tap:tap + seq]
    gate, val = jnp.split(y, 2, axis=-1)
    return (jax.nn.silu(gate) * val) @ w_down

def first_inputs(seed: int = 0) -> dict:
    key = jax.random.key(seed)
    ks = iter(list(jax.random.split(key, 32)))

    def w(shape, fan_in):
        return jax.random.normal(next(ks), shape, jnp.float32) * fan_in ** -0.5

    def gain(shape):
        return 1.0 + 0.1 * jax.random.normal(next(ks), shape, jnp.float32)

    n_a, n_b, n_c, n_d = (_n_layers_of(m) for m in range(N_MIXERS))
    hd = N_HEADS * HEAD_DIM
    x = jax.random.normal(next(ks), (BATCH, SEQ, D_MODEL), jnp.float32)
    offset = jax.random.randint(next(ks), (BATCH, 1), 0, 4096, dtype=jnp.int32)
    positions = offset + jnp.arange(SEQ, dtype=jnp.int32)[None, :]
    return {
        'x': x,
        'positions': positions,
        'mix_norm': gain((DEPTH, D_MODEL)),
        'ffn_norm': gain((DEPTH, D_MODEL)),
        'fox_w_in': w((n_a, D_MODEL, 3 * hd + N_HEADS), D_MODEL),
        'fox_b_f': FOX_FGATE_BIAS + 0.5 * jax.random.normal(next(ks), (n_a, N_HEADS), jnp.float32),
        'fox_q_gain': gain((n_a, HEAD_DIM)),
        'fox_k_gain': gain((n_a, HEAD_DIM)),
        'fox_w_out': w((n_a, hd, D_MODEL), hd),
        'mla_w_in': w((n_b, D_MODEL, MLA_Q_RANK + MLA_KV_RANK + MLA_ROPE), D_MODEL),
        'mla_q_a_gain': gain((n_b, MLA_Q_RANK)),
        'mla_kv_a_gain': gain((n_b, MLA_KV_RANK)),
        'mla_w_q_b': w((n_b, MLA_Q_RANK, N_HEADS * (MLA_NOPE + MLA_ROPE)), MLA_Q_RANK),
        'mla_w_kv_b': w((n_b, MLA_KV_RANK, N_HEADS * (MLA_NOPE + MLA_V)), MLA_KV_RANK),
        'mla_q_gain': gain((n_b, MLA_NOPE + MLA_ROPE)),
        'mla_k_gain': gain((n_b, MLA_NOPE + MLA_ROPE)),
        'mla_w_out': w((n_b, N_HEADS * MLA_V, D_MODEL), N_HEADS * MLA_V),
        'sb_w_in': w((n_c, D_MODEL, 3 * hd), D_MODEL),
        'sb_q_gain': gain((n_c, HEAD_DIM)),
        'sb_k_gain': gain((n_c, HEAD_DIM)),
        'sb_w_out': w((n_c, hd, D_MODEL), hd),
        'sgu_w_in': w((n_d, D_MODEL, 2 * SGU_WIDTH), D_MODEL),
        'sgu_v_gain': gain((n_d, SGU_WIDTH)),
        'sgu_w_s': w((n_d, SGU_GROUPS, SGU_CHUNK, SGU_CHUNK), SGU_CHUNK),
        'sgu_b_s': gain((n_d, SGU_GROUPS, SGU_CHUNK)),
        'sgu_w_out': w((n_d, SGU_WIDTH, D_MODEL), SGU_WIDTH),
        'ffn_w_up': w((DEPTH, D_MODEL, 2 * D_FF), D_MODEL),
        'ffn_conv_w': w((DEPTH, CONV_WIDTH, 2 * D_FF), CONV_WIDTH),
        'ffn_conv_b': 0.01 * jax.random.normal(next(ks), (DEPTH, 2 * D_FF), jnp.float32),
        'ffn_w_down': w((DEPTH, D_FF, D_MODEL), D_FF),
    }

def first_block(x, positions, mix_norm, ffn_norm,
              fox_w_in, fox_b_f, fox_q_gain, fox_k_gain, fox_w_out,
              mla_w_in, mla_q_a_gain, mla_kv_a_gain, mla_w_q_b, mla_w_kv_b,
              mla_q_gain, mla_k_gain, mla_w_out,
              sb_w_in, sb_q_gain, sb_k_gain, sb_w_out,
              sgu_w_in, sgu_v_gain, sgu_w_s, sgu_b_s, sgu_w_out,
              ffn_w_up, ffn_conv_w, ffn_conv_b, ffn_w_down):
    h = x
    for i in range(DEPTH):
        m, j = i % N_MIXERS, i // N_MIXERS
        a = rms_norm(h, mix_norm[i])
        if m == 0:
            mixed = fox_mixer(a, fox_w_in[j], fox_b_f[j], fox_q_gain[j], fox_k_gain[j], fox_w_out[j])
        elif m == 1:
            mixed = mla_mixer(a, positions, mla_w_in[j], mla_q_a_gain[j], mla_kv_a_gain[j],
                              mla_w_q_b[j], mla_w_kv_b[j], mla_q_gain[j], mla_k_gain[j], mla_w_out[j])
        elif m == 2:
            mixed = stick_breaking_mixer(a, sb_w_in[j], sb_q_gain[j], sb_k_gain[j], sb_w_out[j])
        else:
            mixed = sgu_mixer(a, sgu_w_in[j], sgu_v_gain[j], sgu_w_s[j], sgu_b_s[j], sgu_w_out[j])
        h = h + mixed
        h = h + conv_ffn(rms_norm(h, ffn_norm[i]), ffn_w_up[i], ffn_conv_w[i], ffn_conv_b[i], ffn_w_down[i])
    return h


CHUNK = 64
HG_HEADS = 8
HG_DK = 128
HG_DV = 128
HG_WIDTH = HG_HEADS * HG_DV
AT_HEADS = 16
AT_DH = 64
AT_WIDTH = AT_HEADS * AT_DH
LEFT_CHUNKS = 8
BAND = (LEFT_CHUNKS + 1) * CHUNK
REL_CLIP = 256
N_REL = 2 * REL_CLIP + 1
D_FF_2 = 4 * D_MODEL
N_BRANCH = 2
D_IN = 4 * HG_WIDTH + 3 * AT_WIDTH + N_BRANCH * D_MODEL
SPLIT_POINTS = (HG_WIDTH, 2 * HG_WIDTH, 3 * HG_WIDTH, 4 * HG_WIDTH,
                4 * HG_WIDTH + AT_WIDTH, 4 * HG_WIDTH + 2 * AT_WIDTH, 4 * HG_WIDTH + 3 * AT_WIDTH)


def rms_norm_2(x, w):
    xf = x.astype(jnp.float32)
    y = xf * lax.rsqrt(jnp.mean(xf * xf, axis=-1, keepdims=True) + EPS)
    return (y * w.astype(jnp.float32)).astype(x.dtype)

def hgrn2_scan(q, k, v, log_g):
    B, H, T, DK = q.shape
    DV = v.shape[-1]
    nc = T // CHUNK

    def to_chunks(a):
        return a.reshape(B, H, nc, CHUNK, a.shape[-1]).transpose(2, 0, 1, 3, 4)

    causal = jnp.tril(jnp.ones((CHUNK, CHUNK), dtype=bool))

    def step(S, inp):
        qc, kc, vc, gc = inp
        b = jnp.cumsum(gc, axis=2)
        o_inter = jnp.einsum('bhtk,bhkv->bhtv', qc * jnp.exp(b), S)
        diff = b[:, :, :, None, :] - b[:, :, None, :, :]
        decay = jnp.exp(jnp.where(causal[:, :, None], diff, -jnp.inf))
        scores = jnp.einsum('bhtk,bhtsk,bhsk->bhts', qc, decay, kc)
        o_intra = jnp.einsum('bhts,bhsv->bhtv', scores, vc)
        b_last = b[:, :, -1:, :]
        S_new = jnp.exp(b_last[:, :, 0, :])[..., None] * S + jnp.einsum(
            'bhsk,bhsv->bhkv', kc * jnp.exp(b_last - b), vc)
        return S_new, o_inter + o_intra

    S0 = jnp.zeros((B, H, DK, DV), jnp.float32)
    _, o = lax.scan(step, S0, (to_chunks(q), to_chunks(k), to_chunks(v), to_chunks(log_g)))
    return o.transpose(1, 2, 0, 3, 4).reshape(B, H, T, DV)

def chunk_band_attention(q, k, v, rel_bias):
    B, H, T, Dh = q.shape
    nc = T // CHUNK
    pad = LEFT_CHUNKS * CHUNK
    kp = jnp.pad(k, ((0, 0), (0, 0), (pad, 0), (0, 0)))
    vp = jnp.pad(v, ((0, 0), (0, 0), (pad, 0), (0, 0)))
    idx = (jnp.arange(nc) * CHUNK)[:, None] + jnp.arange(BAND)[None, :]
    kb = kp[:, :, idx, :]
    vb = vp[:, :, idx, :]
    qc = q.reshape(B, H, nc, CHUNK, Dh)
    valid = idx >= pad
    t = jnp.arange(CHUNK)
    j = jnp.arange(BAND)
    rel = t[:, None] + pad - j[None, :]
    rel_idx = jnp.clip(rel, -REL_CLIP, REL_CLIP) + REL_CLIP
    bias = rel_bias[:, rel_idx].astype(jnp.float32)
    s = jnp.einsum('bhnqd,bhnkd->bhnqk', qc, kb).astype(jnp.float32) * (Dh ** -0.5) + bias[:, None]
    s = jnp.where(valid[:, None, :], s, -jnp.inf)
    p = jax.nn.softmax(s, axis=-1).astype(v.dtype)
    o = jnp.einsum('bhnqk,bhnkd->bhnqd', p, vb)
    return o.reshape(B, H, T, Dh)

def mixer_block(u, w_in, lb, hg_norm_w, rel_bias, w_branch_a, w_branch_b, w_out):
    B, T, _ = u.shape
    z = u @ w_in
    hq, hf, hi, hg, aq, ak, av, gates = jnp.split(z, SPLIT_POINTS, axis=-1)

    def to_heads(a, h):
        return a.reshape(B, T, h, -1).transpose(0, 2, 1, 3)

    f = jax.nn.sigmoid(hf.astype(jnp.float32))
    g = lb + (1.0 - lb) * f
    log_g = jnp.log(g)
    kk = 1.0 - g
    q = jax.nn.silu(hq.astype(jnp.float32)) * (HG_DK ** -0.5)
    o = hgrn2_scan(to_heads(q, HG_HEADS), to_heads(kk, HG_HEADS),
                   to_heads(hi.astype(jnp.float32), HG_HEADS), to_heads(log_g, HG_HEADS))
    o = o.transpose(0, 2, 1, 3)
    o = rms_norm_2(o, hg_norm_w) * jax.nn.silu(hg.reshape(B, T, HG_HEADS, HG_DV).astype(jnp.float32))
    y_a = o.reshape(B, T, HG_WIDTH).astype(u.dtype)

    ya = chunk_band_attention(to_heads(aq, AT_HEADS), to_heads(ak, AT_HEADS),
                              to_heads(av, AT_HEADS), rel_bias)
    y_b = ya.transpose(0, 2, 1, 3).reshape(B, T, AT_WIDTH)

    gate_a, gate_b = jnp.split(jax.nn.sigmoid(gates), 2, axis=-1)
    merged = gate_a * (y_a @ w_branch_a) + gate_b * (y_b @ w_branch_b)
    return merged @ w_out

def second_inputs(seed: int = 0) -> dict:
    key = jax.random.key(seed)
    ks = jax.random.split(key, 13)
    f32 = jnp.float32
    x = jax.random.normal(ks[0], (BATCH, SEQ, D_MODEL), f32)
    w_in = jax.random.normal(ks[1], (DEPTH, D_MODEL, D_IN), f32) * D_MODEL ** -0.5
    lb_logits = jax.random.normal(ks[2], (DEPTH + 1, HG_WIDTH), f32)
    hg_norm_w = 1.0 + 0.02 * jax.random.normal(ks[3], (DEPTH, HG_DV), f32)
    rel_bias = 0.1 * jax.random.normal(ks[4], (DEPTH, AT_HEADS, N_REL), f32)
    w_branch_a = jax.random.normal(ks[5], (DEPTH, HG_WIDTH, D_MODEL), f32) * HG_WIDTH ** -0.5
    w_branch_b = jax.random.normal(ks[6], (DEPTH, AT_WIDTH, D_MODEL), f32) * AT_WIDTH ** -0.5
    w_out = jax.random.normal(ks[7], (DEPTH, D_MODEL, D_MODEL), f32) * D_MODEL ** -0.5
    norm_mix_w = 1.0 + 0.02 * jax.random.normal(ks[8], (DEPTH, D_MODEL), f32)
    norm_mlp_w = 1.0 + 0.02 * jax.random.normal(ks[9], (DEPTH, D_MODEL), f32)
    w_up = jax.random.normal(ks[10], (DEPTH, D_MODEL, D_FF_2), f32) * D_MODEL ** -0.5
    w_down = jax.random.normal(ks[11], (DEPTH, D_FF_2, D_MODEL), f32) * D_FF_2 ** -0.5
    norm_final_w = 1.0 + 0.02 * jax.random.normal(ks[12], (D_MODEL,), f32)
    return {"x": x, "w_in": w_in, "lb_logits": lb_logits, "hg_norm_w": hg_norm_w,
            "rel_bias": rel_bias, "w_branch_a": w_branch_a, "w_branch_b": w_branch_b,
            "w_out": w_out, "norm_mix_w": norm_mix_w, "norm_mlp_w": norm_mlp_w,
            "w_up": w_up, "w_down": w_down, "norm_final_w": norm_final_w}

def second_block(x, w_in, lb_logits, hg_norm_w, rel_bias, w_branch_a, w_branch_b, w_out,
              norm_mix_w, norm_mlp_w, w_up, w_down, norm_final_w):
    lb_all = jnp.cumsum(jax.nn.softmax(lb_logits.astype(jnp.float32), axis=0), axis=0)
    h = x
    for l in range(DEPTH):
        h = h + mixer_block(rms_norm_2(h, norm_mix_w[l]), w_in[l], lb_all[l], hg_norm_w[l],
                            rel_bias[l], w_branch_a[l], w_branch_b[l], w_out[l])
        u = rms_norm_2(h, norm_mlp_w[l])
        h = h + jnp.square(jax.nn.relu(u @ w_up[l])) @ w_down[l]
    return rms_norm_2(h, norm_final_w)


def setup_inputs(seed=0):
    out = dict(first_inputs(seed))
    for name, value in second_inputs(seed + 1).items():
        if name != "x":
            out[name + "_2"] = value
    return out


def reference(
    x, positions, mix_norm, ffn_norm, fox_w_in, fox_b_f, fox_q_gain, fox_k_gain, fox_w_out,
    mla_w_in, mla_q_a_gain, mla_kv_a_gain, mla_w_q_b, mla_w_kv_b, mla_q_gain, mla_k_gain,
    mla_w_out, sb_w_in, sb_q_gain, sb_k_gain, sb_w_out, sgu_w_in, sgu_v_gain, sgu_w_s, sgu_b_s,
    sgu_w_out, ffn_w_up, ffn_conv_w, ffn_conv_b, ffn_w_down, w_in_2, lb_logits_2, hg_norm_w_2,
    rel_bias_2, w_branch_a_2, w_branch_b_2, w_out_2, norm_mix_w_2, norm_mlp_w_2, w_up_2,
    w_down_2, norm_final_w_2,
):
    x = first_block(
        x, positions, mix_norm, ffn_norm, fox_w_in, fox_b_f, fox_q_gain, fox_k_gain, fox_w_out,
        mla_w_in, mla_q_a_gain, mla_kv_a_gain, mla_w_q_b, mla_w_kv_b, mla_q_gain, mla_k_gain,
        mla_w_out, sb_w_in, sb_q_gain, sb_k_gain, sb_w_out, sgu_w_in, sgu_v_gain, sgu_w_s,
        sgu_b_s, sgu_w_out, ffn_w_up, ffn_conv_w, ffn_conv_b, ffn_w_down,
    )
    return second_block(
        x, w_in_2, lb_logits_2, hg_norm_w_2, rel_bias_2, w_branch_a_2, w_branch_b_2, w_out_2,
        norm_mix_w_2, norm_mlp_w_2, w_up_2, w_down_2, norm_final_w_2,
    )


_drawn_inputs = setup_inputs


def setup_inputs(seed=0):
    import zlib

    import numpy as np

    out = dict(_drawn_inputs(seed))
    spreads = {}
    factors = {'ffn_conv_b': 7.111,
     'hg_norm_w_2': 25.502,
     'rel_bias_2': 24.554,
     'norm_mix_w_2': 6.469,
     'norm_mlp_w_2': 16.437,
     'norm_final_w_2': 7.393}
    for name, (base, spread) in spreads.items():
        noise = np.random.default_rng([zlib.crc32(name.encode()), seed]).standard_normal(out[name].shape)
        drawn = base * np.exp(spread * noise) if base else spread * noise
        out[name] = __import__('jax').numpy.asarray(drawn.astype(out[name].dtype))
    for name, factor in factors.items():
        out[name] = (out[name] * factor).astype(out[name].dtype)
    return out
```

```python
from contextlib import ExitStack

import numpy as np

import concourse.bass as bass
from concourse import mybir

ALU = mybir.AluOpType
ACT = mybir.ActivationFunctionType
AX_X = mybir.AxisListType.X
F32 = mybir.dt.float32
F32R = mybir.dt.float32r
U8 = mybir.dt.uint8

P = 128
T = 256
TT = T // P
D = 2048
KT = D // P
EPS = 1e-6
BIG = 1e30

CW = 512
JT = CW // P
RING = 4
AHEAD = RING - 1
SLOT_K = 2
SPC = KT // SLOT_K
NCH = D // CW

FOX_H = 16
GROUPS = FOX_H // JT
D_FF = 5632
FFN1 = D_FF // CW
HG_H = 8
HG_W = HG_H * P
AT_H = 16
AT_D = 64
AT_W = AT_H * AT_D
REL = 256
LEVELS = 8
D_FF_2 = 4 * D
FFN2 = D_FF_2 // CW

C_ID, C_MIRROR, C_CAUSAL, C_BAND, C_SEL, C_AUG, C_END = 0, 128, 256, 512, 768, 784, 790
G_MIX, G_FFN, G_MIX2, G_MLP2, G_FQ, G_FK, G_LB, G_END = 0, 16, 32, 48, 64, 65, 66, 82


def constants():
    r = np.arange(P)
    c = np.zeros((P, C_END), np.float32)
    c[:, C_ID:C_ID + P] = np.eye(P)
    c[:, C_MIRROR:C_MIRROR + P] = -np.eye(P)[::-1]
    c[:, C_CAUSAL + P:C_CAUSAL + 2 * P] = BIG * (r[None, :] > r[:, None])
    c[:, C_BAND + P:C_BAND + 2 * P] = BIG * (r[None, :] // 64 > r[:, None] // 64)
    for h in range(FOX_H):
        c[h:4 * FOX_H:FOX_H, C_SEL + h] = 1
    rows = np.arange(P) // FOX_H
    for col, group, v in ((0, 0, 1), (1, 1, 1), (2, 2, 1), (2, 3, 1), (3, 2, 1), (4, 3, 1), (5, 0, -1), (5, 1, -1)):
        c[rows == group, C_AUG + col] = v
    until = np.zeros((P, 2 * P), np.float32)
    until[:, :P] = r[:, None] <= r[None, :]
    until[:, P:] = 1
    levels = np.zeros((P, LEVELS, P), np.float32)
    levels[:, 0] = r[:, None] == r[None, :]
    for k in range(1, LEVELS):
        h = 1 << (k - 1)
        s, t = r[:, None], r[None, :]
        levels[:, k] = (s // (2 * h) == t // (2 * h)) & (s // h % 2 == 0) & (t // h % 2 == 1)
    return c, until, levels.reshape(P, LEVELS * P)


class Chain:

    def __init__(self, eng, sem):
        self.eng, self.sem, self.base, self.n = eng, sem, 0, 0

    def link(self, ins):
        ins.then_inc(self.sem, 1)
        self.n += 1
        self.eng.wait_ge(self.sem, self.base + self.n)

    def enter(self, i, first, per):
        self.start, self.per = self.n, per
        self.base, self.n = (i - first) * per + self.start, 0

    def leave(self, passes):
        assert self.n == self.per, (self.n, self.per)
        self.base, self.n = 0, self.start + passes * self.per


def build_program(nc, a, out):
    with ExitStack() as ctx:
        def sb(name, shape, dt=F32):
            return ctx.enter_context(nc.sbuf_tensor(name, shape, dt))

        def sem(name):
            return ctx.enter_context(nc.semaphore(name))

        raw = sb("raw", [P, RING, SLOT_K * CW])
        w_hi = sb("w_hi", [P, RING, SLOT_K * CW], F32R)
        w_lo = sb("w_lo", [P, RING, SLOT_K * CW], F32R)
        A_hi, A_lo = sb("A_hi", [P, KT, T], F32R), sb("A_lo", [P, KT, T], F32R)
        B_hi, B_lo = sb("B_hi", [P, KT, T], F32R), sb("B_lo", [P, KT, T], F32R)
        C_hi, C_lo = sb("C_hi", [P, JT, T], F32R), sb("C_lo", [P, JT, T], F32R)
        resid = sb("resid", [P, TT, D])
        const = sb("const", [P, C_END])
        levels = sb("levels", [P, LEVELS, P], U8)
        gain = sb("gain", [P, G_END])
        conv = sb("conv", [P, 4, 2 * D_FF // P])
        hg_gain = sb("hg_gain", [P, P])
        pT = sb("pT", [P, 3 * P])
        junk = sb("junk", [P, CW])
        small = sb("small", [P, 144])
        scratch = sb("scratch", [P, 15, 1024])
        ident = const[:, C_ID:C_ID + P]

        def unit(k):
            return scratch[:, k, :]

        rstd = small[:, 0:2]
        nothalf, eps = small[:, 2:10], small[:, 10:18]
        ssq = small[:, 18:26]
        ssum = small[:, 26:28]
        head_ss = small[:, 28:36]
        head_rs = small[:, 36:44]
        fq_scale = small[:, 44:45]
        least = small[:, 46:50]
        psums = small[:, 50:54]
        precip = small[:, 54:58]
        lbnd = small[:, 58:66]
        one_lb = small[:, 66:74]
        lb_tmp = small[:, 74:98]
        f_bias = small[:, 98:114]
        mean_t = small[:, 130:138]
        wait_slot = small[:, 143:144]

        acc = ctx.enter_context(nc.psum_tensor("acc", [P, 8, CW], F32))
        BK = [(0, 1), (2, 3), (4, 5), (6, 7)]
        D1_BANKS = [BK[0], BK[1], BK[0], BK[3]]
        D2_BANKS, D2_LAST = [BK[1], BK[3], BK[0], BK[1]], [BK[0], BK[3], BK[1], BK[0]]
        turn_ps = acc[:, 4:6, :].rearrange("p b c -> p (b c)")
        pair3 = acc[:, 6:8, :].rearrange("p b c -> p (b c)")

        landed = [sem(f"landed{i}") for i in range(RING)]
        w_hi_ready, w_lo_ready, slot_done = sem("w_hi_ready"), sem("w_lo_ready"), sem("slot_done")
        x_in = [sem(f"x_in{c}") for c in range(NCH)]
        ident_in, const_in, tab_in, f_kept = sem("ident_in"), sem("const_in"), sem("tab_in"), sem("f_kept")
        f_in, late_in, level_in, gain_in = sem("f_in"), sem("late_in"), sem("level_in"), sem("gain_in")
        bias_in = [sem("bias_in0"), sem("bias_in1")]
        lb_shift, lb_exp, f_z = sem("lb_shift"), sem("lb_exp"), sem("f_z")
        product, gated_hi, squared, merge_read = sem("product"), sem("gated_hi"), sem("squared"), sem("merge_read")
        hg_gated = sem("hg_gated")
        out_sent, hg_gain_in, levels_made = sem("out_sent"), sem("hg_gain_in"), sem("levels_made")
        tabs_turned, tabs_kept, f_turned = sem("tabs_turned"), sem("tabs_kept"), sem("f_turned")
        f_hi, f_lo = sem("f_hi"), sem("f_lo")
        z1_half, z1_first = sem("z1_half"), sem("z1_first")
        turned, turn_act, turn_dve = sem("turned"), sem("turn_act"), sem("turn_dve")
        squares, sums, rstd_ready = sem("squares"), sem("sums"), sem("rstd_ready")
        z1_out, res1_out, up1_out, down1_out = sem("z1_out"), sem("res1_out"), sem("up1_out"), sem("down1_out")
        z2_out, merged_out, res2_out = sem("z2_out"), sem("merged_out"), sem("res2_out")
        up2_out, down2_out = sem("up2_out"), sem("down2_out")
        head_sums, head_rstd, head_normed = sem("head_sums"), sem("head_rstd"), sem("head_normed")
        f_log, log_f, cum_turned, cum_kept = (
            sem("f_log"), sem("log_f"), sem("cum_turned"), sem("cum_kept"))
        gates_row, qk_turned, qk_kept = sem("gates_row"), sem("qk_turned"), sem("qk_kept")
        scored, masked, exped, probs = sem("scored"), sem("masked"), sem("exped"), sem("probs")
        probs_turned, probs_kept, mixed = sem("probs_turned"), sem("probs_kept"), sem("mixed")
        mixed_hi, mixed_lo = sem("mixed_hi"), sem("mixed_lo")
        gate_sig, gated = sem("gate_sig"), sem("gated")
        zeroed, filled = sem("zeroed"), sem("filled")
        lv_ready, lv_done, lv_kept = sem("lv_ready"), sem("lv_done"), sem("lv_kept")
        hg_mixed, hg_square, hg_sums, hg_rstd, hg_normed = (
            sem("hg_mixed"), sem("hg_square"), sem("hg_sums"), sem("hg_rstd"), sem("hg_normed"))
        hg_sig, gate2_sig = sem("hg_sig"), sem("gate2_sig")
        final_ready, gained = [sem("final_ready0"), sem("final_ready1")], sem("gained")
        act_self, dve_self, pool_self = sem("act_self"), sem("dve_self"), sem("pool_self")

        block = ctx.enter_context(nc.Block())

        def rounds(slots):
            assert slots % RING == 0
            return slots // RING

        R1 = 0
        R2 = R1 + rounds(3 * GROUPS * SPC)
        R3 = R2 + rounds(NCH * SPC)
        B3 = rounds(2 * SPC + NCH * JT // SLOT_K)
        R4 = R3 + FFN1 * B3
        Z2 = 22
        R5 = R4 + rounds(Z2 * SPC)
        R6 = R5 + rounds(NCH * SPC)
        R7 = R6 + rounds(NCH * SPC)
        B7 = rounds(SPC + NCH * JT // SLOT_K)
        R_END = R7 + FFN2 * B7
        F1 = rounds(3 * SPC)
        U1 = rounds(2 * SPC)
        U2 = rounds(SPC)

        TN_X, TN_RES1, TN_FFN1, TN_DOWN1 = 0, 4, 8, 8 + 2 * FFN1
        TN_HG = TN_DOWN1 + 4
        TN_MERGE, TN_RES2, TN_FFN2 = TN_HG + 6, TN_HG + 10, TN_HG + 14

        OUT1 = ([(0, k) for k in range(6)] + [(1, k) for k in range(6)] + [(0, 6), (0, 7), (1, 6), (1, 7)]
                + [(c, k) for c in (2, 3) for k in range(8)])
        OUT1_END = [14, 16, 24, 32]

        GATE_COL = [4 * HG_W + 3 * AT_W + k * CW for k in range(8)]
        Z2_COL = ([k * HG_W + g * CW for g in range(2) for k in range(4)]
                  + [4 * HG_W + k * AT_W for k in range(3)] + GATE_COL[:3]
                  + [4 * HG_W + k * AT_W + CW for k in range(3)] + GATE_COL[3:])
        HG_AT = [18, 54]
        AT_AT = [92, 132]

        def hg_step(p):
            for g, b in enumerate(HG_AT):
                if p == b:
                    return g, "turn_q", 0
                if p == b + 2:
                    return g, "turn_f", 0
                if 0 <= p - b - 4 <= 3 * LEVELS and (p - b - 4) % 3 == 0:
                    return g, "level", (p - b - 4) // 3
                if p == b + 31:
                    return g, "mix", 0
                if p == b + 34:
                    return g, "turn_y", 0
            return None

        def at_steps(p):
            steps = []
            for g, b in enumerate(AT_AT):
                for j in range(8):
                    for kind, at in (("mix", 2 * j + 5), ("turn_p", 2 * j + 3), ("score", 2 * j + 1)):
                        if p == b + at:
                            steps.append((kind, g, j))
                for j in range(0, 8, 2):
                    if p == b + 2 * j - 1:
                        steps.append(("turn_qk", g, j))
            return steps

        def fox_steps(p, last=False):
            at = {"mix": 5, "turn_p": 3, "score": 1, "turn_qk": 0} if last else \
                 {"mix": 8, "turn_p": 5, "score": 3, "turn_qk": 1}
            return [(kind, j) for kind in ("mix", "turn_p", "score", "turn_qk") for j in range(JT)
                    if p == 2 * j + at[kind]]

        stage_q, stage_k = unit(0), unit(1)
        v_sb, sq_sb = unit(2), unit(3)
        qT, kT = unit(4)[:, 0:T], unit(4)[:, T:2 * T]
        cum_l, cum_t = unit(5)[:, 0:T], unit(5)[:, T:2 * T]
        logf = unit(5)[:, 2 * T:3 * T].rearrange("p (t c) -> p t c", t=TT)
        until = unit(5)[:, 3 * T:4 * T]
        fw_raw = unit(6)[:, 0:256]
        f_lin = unit(6)[0:FOX_H, 320:320 + T]
        f_logit, f_abs = unit(6)[:, 256:288], unit(6)[:, 288:320]
        fw_hi, fw_lo = (c[:, 0, :].rearrange("p (k n) -> p k n", k=KT) for c in (C_hi, C_lo))
        row_l, cum_r, cum_hi, cum_lo = C_hi[:, 1:3, :], C_hi[:, 3, :], C_lo[:, 1, :], C_lo[:, 2, :]
        prob = unit(7)[:, 0:768].rearrange("p (b c) -> p b c", b=2)
        tabs = unit(8)[:, 0:5 * P].rearrange("p (k c) -> p k c", k=5)
        g_T, u_T, s_T = unit(1), unit(2), unit(3)
        v_pad = scratch[:, 2:4, :].rearrange("p t (h d) -> p t h d", d=P)
        bias_T = scratch[:, 4:6, :].rearrange("p u c -> p (u c)").rearrange("p (h t) -> p h t", t=T)
        q2T, k2T = unit(6)[:, 0:T], unit(6)[:, T:3 * T].rearrange("p (u t) -> p u t", u=2)
        h_q, h_k, run, rest = unit(4), unit(5), unit(6), unit(7)
        h_v, h_g = unit(8), unit(9)
        Z = [unit(10), unit(11)]
        near, far = unit(12), unit(13)[:, 0:CW]
        GATE_U = [8, 9, 10, 11, 12, 13, 14, 4]
        gain_out = scratch[:, 4:6, :].rearrange("p u c -> p (u c)")

        @block.sync
        def _(sp):
            x = a["x"].rearrange("b (t p) d -> p (b t) d", p=P)

            def load(R, p, w, row, col, wait=True):
                ring = p % RING
                if wait:
                    sp.wait_ge(w_lo_ready, RING * R + p - AHEAD)
                src = w[row:row + SLOT_K * P, bass.ds(col, CW)].rearrange("(k p) n -> p k n", p=P)
                sp.dma_start(raw[:, ring, :].rearrange("p (k n) -> p k n", k=SLOT_K), src).then_inc(landed[ring], 16)

            def fox_body(R, g, first=False):
                for k in range(3):
                    for s in range(SPC):
                        p = k * SPC + s
                        if first and p < NCH:
                            c = slice(p * CW, (p + 1) * CW)
                            sp.dma_start(resid[:, :, c], x[:, :, c]).then_inc(x_in[p], 16)
                        load(R, p, a["w1"], s * SLOT_K * P, g * CW + k * D, wait=not (first and p < RING))

            fox_body(R1, 0, first=True)
            with sp.Fori(1, GROUPS) as g:
                fox_body(R1 + F1 * g, g)
            for p, (c, k) in enumerate(OUT1):
                load(R2, p, a["wo1"], k * SLOT_K * P, c * CW)

            def ups1(R, i):
                for k in range(2):
                    for s in range(SPC):
                        load(R, k * SPC + s, a["up1"], s * SLOT_K * P, i * CW + k * D_FF)

            def downs(R, p0, w, i):
                for n in range(NCH):
                    for s in range(JT // SLOT_K):
                        rows = w[bass.ds(i * CW + s * SLOT_K * P, SLOT_K * P), n * CW:(n + 1) * CW]
                        p = p0 + n * (JT // SLOT_K) + s
                        sp.wait_ge(w_lo_ready, RING * R + p - AHEAD)
                        sp.dma_start(raw[:, p % RING, :].rearrange("p (k n) -> p k n", k=SLOT_K),
                                     rows.rearrange("(k p) n -> p k n", p=P)).then_inc(landed[p % RING], 16)

            ups1(R3, 0)
            with sp.Fori(1, FFN1) as i:
                R = R3 + U1 + B3 * (i - 1)
                ups1(R, i)
                downs(R, 2 * SPC, a["down1"], i - 1)
            downs(R4 - 2, 0, a["down1"], FFN1 - 1)
            for c, col in enumerate(Z2_COL):
                for s in range(SPC):
                    load(R4, c * SPC + s, a["w2"], s * SLOT_K * P, col)
            for n in range(NCH):
                for s in range(SPC):
                    w, r = (a["wa"], s) if s < SPC // 2 else (a["wb"], s - SPC // 2)
                    load(R5, n * SPC + s, w, r * SLOT_K * P, n * CW)
            for n in range(NCH):
                for s in range(SPC):
                    load(R6, n * SPC + s, a["wo2"], s * SLOT_K * P, n * CW)

            def ups2(R, i):
                for s in range(SPC):
                    load(R, s, a["up2"], s * SLOT_K * P, i * CW)

            ups2(R7, 0)
            with sp.Fori(1, FFN2) as i:
                R = R7 + U2 + B7 * (i - 1)
                ups2(R, i)
                downs(R, SPC, a["down2"], i - 1)
            downs(R_END - 2, 0, a["down2"], FFN2 - 1)
            o = out.rearrange("b (t p) d -> p (b t) d", p=P)
            for k in range(2 * TT):
                t, v = k % 2, slice(k // 2 * D // 2, (k // 2 + 1) * D // 2)
                sp.wait_ge(final_ready[t], k // 2 + 1)
                sp.dma_start(o[:, t, v], resid[:, t, v]).then_inc(out_sent, 16)
            sp.wait_ge(out_sent, 2 * TT * 16)

        @block.tensor
        def _(pe):
            def gemm(R, p, hi, lo, kp, banks, first, last, late=None, half=None):
                pe.wait_ge(w_lo_ready, RING * R + p + 1)
                ring = p % RING
                for t in range(TT):
                    if late and t == 1:
                        pe.wait_ge(*late)
                    for kk in range(SLOT_K):
                        kt = kp * SLOT_K + kk
                        wh, wl = (w[:, ring, kk * CW:(kk + 1) * CW] for w in (w_hi, w_lo))
                        o, ts = acc[:, banks[t], :], slice(t * P, (t + 1) * P)
                        pe.matmul(o, hi[:, kt, ts], wh, start=first and kk == 0, stop=False)
                        pe.matmul(o, hi[:, kt, ts], wl, start=False, stop=False)
                        m = pe.matmul(o, lo[:, kt, ts], wh, start=False, stop=last and kk == SLOT_K - 1)
                    if half and t == 0:
                        m.then_inc(half, 1)
                m.then_inc(slot_done, 1)

            def turn(src, n):
                pe.wait_ge(turn_act, n)
                pe.wait_ge(turn_dve, n)
                for j in range(JT):
                    for t in range(TT):
                        m = pe.transpose(turn_ps[:, j * T + t * P:j * T + (t + 1) * P], src(t, j), ident)
                m.then_inc(turned, 1)

            def halves(u):
                return lambda t, j: u[:, t * CW + j * P:t * CW + (j + 1) * P]

            def chunk_of_resid(c):
                return lambda t, j: resid[:, t, c * CW + j * P:c * CW + (j + 1) * P]

            pe.wait_ge(ident_in, 16)
            pe.wait_ge(tab_in, 16)
            for k, (rows, col) in enumerate([(G_END, 0)] + [(88, P * (1 + k)) for k in range(4)]):
                m = pe.transpose(acc[:, 6 + k // 4, (col % CW):(col % CW) + rows], tabs[0:rows, k, :],
                                 ident[0:rows, 0:rows])
            m.then_inc(tabs_turned, 1)

            def first_steps(p):
                if p == 0:
                    pe.wait_ge(x_in[0], 16)
                    turn(chunk_of_resid(0), TN_X)
                if p < 6 and p % 2 == 0:
                    c = p // 2 + 1
                    pe.wait_ge(x_in[c], 16)
                    turn(chunk_of_resid(c), TN_X + c)
                if p == 6:
                    pe.wait_ge(turn_dve, NCH)
                if p == 9:
                    pe.wait_ge(f_lo, 1)
                    pe.wait_ge(tabs_kept, 1)
                    o = acc[0:FOX_H, 6, 0:T]
                    for kt in range(KT):
                        pe.matmul(o, fw_hi[:, kt, :], A_hi[:, kt, :], start=kt == 0, stop=False)
                        pe.matmul(o, fw_lo[:, kt, :], A_hi[:, kt, :], start=False, stop=False)
                        m = pe.matmul(o, fw_hi[:, kt, :], A_lo[:, kt, :], start=False, stop=kt == KT - 1)
                    m.then_inc(f_turned, 1)
                if p == 11:
                    pe.wait_ge(f_kept, 1)
                    for t in range(TT):
                        m = pe.transpose(acc[:, 6, T + t * FOX_H:T + (t + 1) * FOX_H], f_lin[:, t * P:(t + 1) * P],
                                         ident[0:FOX_H, 0:FOX_H])
                    m.then_inc(f_turned, 1)
                if p == 2 * SPC:
                    cumulate()

            def cumulate():
                pe.wait_ge(log_f, 1)
                pe.wait_ge(late_in, 16)
                pe.matmul(acc[:, 7, 0:T], logf[:, 0, :], until, start=True, stop=False)
                pe.matmul(acc[:, 7, P:T], logf[:, 1, :], until[:, 0:P], start=False, stop=True).then_inc(cum_turned, 1)

            def scores(n, q, k, extra):
                pe.wait_ge(masked, n)
                for t in range(TT):
                    o = acc[:, 6, t * P:t * P + (t + 1) * P]
                    extra(t, o)
                    m = pe.matmul(o, q[:, t * P:(t + 1) * P], k[:, 0:(t + 1) * P], start=False, stop=True)
                m.then_inc(scored, 1)

            def turn_probs(n, buf):
                pe.wait_ge(probs, n + 1)
                pe.wait_ge(probs_kept, n)
                for c in range(3):
                    m = pe.transpose(acc[:, 7, c * P:(c + 1) * P], prob[:, buf, c * P:(c + 1) * P], ident)
                m.then_inc(probs_turned, 1)

            def fox_step(kind, g, j):
                n = JT * g + j
                if kind == "turn_qk":
                    pe.wait_ge(head_normed, 2 * g + 2)
                    pe.wait_ge(qk_kept, n)
                    for k, u in enumerate((stage_q, stage_k)):
                        for t in range(TT):
                            m = pe.transpose(acc[:, 4, k * T + t * P:k * T + (t + 1) * P], halves(u)(t, j), ident)
                    m.then_inc(qk_turned, 1)
                if kind == "score":
                    pe.wait_ge(qk_kept, n + 1)
                    pe.wait_ge(gates_row, n + 1)
                    scores(n, qT, kT, lambda t, o: pe.matmul(
                        o, row_l[:, j % 2, t * P:(t + 1) * P], cum_r[:, 0:(t + 1) * P], start=True, stop=False))
                if kind == "turn_p":
                    turn_probs(n, j % 2)
                if kind == "mix":
                    pe.wait_ge(probs_kept, n + 1)
                    pe.wait_ge(mixed_lo, n)
                    pe.wait_ge(z1_out, 3 * g + 3)
                    v = halves(v_sb)
                    pe.matmul(acc[:, 5, 0:T], v(0, j), pT[:, 0:T], start=True, stop=False)
                    pe.matmul(acc[:, 5, P:T], v(1, j), pT[:, T:T + P], start=False, stop=True).then_inc(mixed, 1)

            def fox_pass(R, g, first=False):
                for p in range(3 * SPC):
                    if first:
                        first_steps(p)
                    else:
                        for kind, j in fox_steps(p):
                            fox_step(kind, g - 1, j)
                    c, s = divmod(p, SPC)
                    late = None
                    if s == 0 and c == 0 and not first:
                        pe.wait_ge(z1_first, 3 * g)
                        late = z1_out, 3 * g
                    if s == 0 and c == 2:
                        pe.wait_ge(z1_out, 3 * g + 1)
                    gemm(R, p, A_hi, A_lo, s, BK[c % 2], s == 0, s == SPC - 1, late, z1_half if s == SPC - 1 else None)

            fox_pass(R1, 0, first=True)
            fox_pass(R1 + F1, 1)
            with pe.Fori(2, GROUPS) as g:
                fox_pass(R1 + F1 * g, g)

            for p, (c, k) in enumerate(OUT1):
                for kind, j in fox_steps(p, last=True):
                    fox_step(kind, GROUPS - 1, j)
                for m in range(NCH - 1):
                    if p == OUT1_END[m] + 2:
                        pe.wait_ge(res1_out, m + 1)
                        pe.wait_ge(mixed_lo, FOX_H)
                        turn(chunk_of_resid(m), TN_RES1 + m)
                late = None
                if k == 0:
                    if c == 0:
                        pe.wait_ge(z1_first, 3 * GROUPS)
                        late = z1_out, 3 * GROUPS
                    elif c > 1:
                        pe.wait_ge(res1_out, c - 1)
                if p == 0:
                    pe.wait_ge(mixed_lo, FOX_H - JT)
                if p == 12:
                    pe.wait_ge(mixed_lo, FOX_H)
                gemm(R2, p, B_hi, B_lo, k, BK[c % 2], k == 0, k == SPC - 1, late)

            def ups1(R, i, first=False):
                for p in range(2 * SPC):
                    c, s = divmod(p, SPC)
                    if first:
                        if p == 0:
                            pe.wait_ge(res1_out, 3)
                            pe.wait_ge(turn_dve, TN_RES1 + 3)
                        if p == 2:
                            pe.wait_ge(res1_out, 4)
                            turn(chunk_of_resid(3), TN_RES1 + 3)
                        if p == 6:
                            pe.wait_ge(turn_dve, TN_RES1 + 4)
                    elif p == 1:
                        pe.wait_ge(up1_out, 2 * i)
                        turn(halves(stage_q), TN_FFN1 + 2 * i - 1)
                    if p == 10:
                        pe.wait_ge(up1_out, 2 * i + 1)
                        turn(halves(stage_q), TN_FFN1 + 2 * i)
                    gemm(R, p, A_hi, A_lo, s, BK[c], s == 0, s == SPC - 1)

            def downs(R, p0, banks, free, ready, steps=None, operand=(C_hi, C_lo)):
                for q in range(2 * NCH):
                    n, s = divmod(q, 2)
                    if steps:
                        steps(q)
                    if q == 0:
                        pe.wait_ge(*ready)
                    if s == 0 and free[n]:
                        pe.wait_ge(*free[n])
                    gemm(R, p0 + q, *operand, s, banks[n], s == 0, s == 1)

            ups1(R3, 0, first=True)

            def pass1(R, i, steps=None):
                ups1(R, i)
                downs(R, 2 * SPC, D1_BANKS, [(up1_out, 2 * i + 1), (up1_out, 2 * i + 2), (down1_out, 4 * i - 3), None],
                      (gated, i), steps)
                pe.wait_ge(down1_out, 4 * i - 1)

            def last_turn1(q):
                if q == 2:
                    pe.wait_ge(up1_out, 2 * FFN1)
                    turn(halves(stage_q), TN_FFN1 + 2 * FFN1 - 1)

            def down1_steps(q):
                if q >= 3 and q % 2 == 1:
                    m = (q - 3) // 2
                    pe.wait_ge(down1_out, 4 * (FFN1 - 1) + m + 1)
                    turn(chunk_of_resid(m), TN_DOWN1 + m)

            with pe.Fori(1, FFN1 - 1) as i:
                pass1(R3 + U1 + B3 * (i - 1), i)
            pass1(R4 - 2 - B3, FFN1 - 1, last_turn1)
            downs(R4 - 2, 0, D1_BANKS, [None, None, (down1_out, 4 * (FFN1 - 1) + 1), None], (gated, FFN1),
                  down1_steps, (B_hi, B_lo))

            def level(g, k):
                n = (LEVELS + 1) * g + k
                o = turn_ps if k % 2 == 0 else pair3
                pe.wait_ge(lv_ready, n + 1)
                if k >= 2:
                    pe.wait_ge(lv_kept, n - 1)
                elif k == 0:
                    pe.wait_ge(turn_dve, TN_HG + 3 * g + 2)
                    pe.wait_ge(turn_act, TN_HG + 3 * g + 2)
                elif g:
                    pe.wait_ge(hg_normed, g)
                if k == LEVELS:
                    z = Z[k % 2]
                    for j in range(JT):
                        m = pe.matmul(o[:, j * P:(j + 1) * P], z[:, j * T:j * T + P], z[:, j * T + P:(j + 1) * T],
                                      start=True, stop=True)
                else:
                    s, t = (h_k, h_q) if k == 0 else (Z[k % 2], Z[k % 2])
                    for b in range(2 * JT):
                        c = slice(b * P, (b + 1) * P)
                        m = pe.matmul(o[:, c], s[:, c], t[:, c], start=True, stop=True)
                m.then_inc(lv_done, 1)

            def hg_mix(g):
                pe.wait_ge(lv_kept, (LEVELS + 1) * (g + 1))
                pe.wait_ge(z2_out, 4 * g + 3)
                v = halves(h_v)
                for j in range(JT):
                    pe.matmul(pair3[:, j * P:(j + 1) * P], near[:, 2 * j * P:(2 * j + 1) * P], v(0, j),
                              start=True, stop=True)
                for j in range(JT):
                    o = pair3[:, CW + j * P:CW + (j + 1) * P]
                    pe.matmul(o, far[:, j * P:(j + 1) * P], v(0, j), start=True, stop=False)
                    m = pe.matmul(o, near[:, (2 * j + 1) * P:(2 * j + 2) * P], v(1, j), start=False, stop=True)
                m.then_inc(hg_mixed, 1)

            def at_step(kind, g, j):
                n = FOX_H + 8 * g + j
                pair = FOX_H + 4 * g + j // 2
                if kind == "turn_qk":
                    pe.wait_ge(z2_out, 8 + 6 * g + 2)
                    pe.wait_ge(qk_kept, pair)
                    pe.wait_ge(turn_dve, TN_HG + 6)
                    pe.wait_ge(turn_act, TN_HG + 6)
                    for k, u in enumerate((stage_q, stage_k)):
                        for t in range(TT):
                            m = pe.transpose(acc[:, 4, k * T + t * P:k * T + (t + 1) * P],
                                             halves(u)(t, j // 2), ident)
                    m.then_inc(qk_turned, 1)
                if kind == "score":
                    pe.wait_ge(qk_kept, pair + 1)
                    pe.wait_ge(bias_in[g], 16)

                    def bias(t, o):
                        for k in range(t + 1):
                            pe.matmul(o[:, k * P:(k + 1) * P], bias_T[:, j, (t - k) * P:(t - k + 1) * P],
                                      const[:, C_MIRROR:C_MIRROR + P], start=k == 0, stop=False)

                    scores(n, q2T, k2T[:, j % 2, :], bias)
                if kind == "turn_p":
                    turn_probs(n, j % 2)
                if kind == "mix":
                    pe.wait_ge(probs_kept, n + 1)
                    pe.wait_ge(z2_out, 8 + 6 * g + 3)
                    if j % 2 == 0:
                        pe.wait_ge(mixed_lo, pair)
                    all_targets = (acc[:, 5, 0:T], v_pad[:, 0, j, :], pT[:, 0:T])
                    late_targets = (acc[:, 5, P:T], v_pad[:, 1, j, :], pT[:, T:T + P])
                    if j % 2 == 0:
                        pe.matmul(*all_targets, start=True, stop=False)
                        pe.matmul(*late_targets, start=False, stop=False).then_inc(mixed, 1)
                    else:
                        pe.matmul(*late_targets, start=False, stop=False)
                        pe.matmul(*all_targets, start=False, stop=True).then_inc(mixed, 1)

            for p in range(Z2 * SPC):
                c, s = divmod(p, SPC)
                if p == 1:
                    pe.wait_ge(down1_out, 4 * FFN1)
                    turn(chunk_of_resid(3), TN_DOWN1 + 3)
                step = hg_step(p)
                if step:
                    g, kind, k = step
                    if kind in ("turn_q", "turn_f"):
                        f = kind == "turn_f"
                        pe.wait_ge(z2_out, 4 * g + 1 + f)
                        turn(halves(stage_k if f else stage_q), TN_HG + 3 * g + f)
                    if kind == "level":
                        level(g, k)
                    if kind == "mix":
                        hg_mix(g)
                    if kind == "turn_y":
                        pe.wait_ge(hg_normed, g + 1)
                        turn(halves(Z[0]), TN_HG + 3 * g + 2)
                for kind, g, j in at_steps(p):
                    at_step(kind, g, j)
                if p == 0:
                    pe.wait_ge(down1_out, 4 * FFN1 - 1)
                    pe.wait_ge(turn_dve, TN_DOWN1 + 3)
                if p == 6:
                    pe.wait_ge(turn_dve, TN_DOWN1 + 4)
                if s == 0 and c >= 2:
                    pe.wait_ge(z2_out, c - 1)
                gemm(R4, p, A_hi, A_lo, s, BK[c % 2], s == 0, s == SPC - 1)

            H = SPC // 2
            for p in range(NCH * SPC):
                n, s = divmod(p, SPC)
                if p == 2 + SPC * n and n:
                    pe.wait_ge(merged_out, n)
                    turn(halves(stage_q), TN_MERGE + n - 1)
                if p == 0:
                    pe.wait_ge(z2_out, Z2 - 1)
                    pe.wait_ge(turn_dve, TN_HG + 6)
                if p == H:
                    pe.wait_ge(z2_out, Z2)
                    pe.wait_ge(mixed_lo, FOX_H + AT_H // 2)
                if s % H == 0 and n:
                    pe.wait_ge(merge_read, 2 * n - 1 + s // H)
                gemm(R5, p, B_hi, B_lo, s, BK[s // H], s % H == 0, s % H == H - 1)
            for p in range(NCH * SPC):
                n, s = divmod(p, SPC)
                if p == 2:
                    pe.wait_ge(merged_out, NCH)
                    turn(halves(stage_q), TN_MERGE + NCH - 1)
                if p == 2 + SPC * n and n:
                    pe.wait_ge(res2_out, n)
                    turn(chunk_of_resid(n - 1), TN_RES2 + n - 1)
                if p == 0:
                    pe.wait_ge(turn_dve, TN_MERGE + 3)
                if p == 6:
                    pe.wait_ge(turn_dve, TN_MERGE + 4)
                if s == 0:
                    if n < 2:
                        pe.wait_ge(merge_read, 2 * NCH - 1 + n)
                    else:
                        pe.wait_ge(res2_out, n - 1)
                gemm(R6, p, A_hi, A_lo, s, BK[n % 2], s == 0, s == SPC - 1)

            def ups2(R, i, first=False):
                for p in range(SPC):
                    if first:
                        if p == 0:
                            pe.wait_ge(res2_out, 3)
                            pe.wait_ge(turn_dve, TN_RES2 + 3)
                        if p == 2:
                            pe.wait_ge(res2_out, 4)
                            turn(chunk_of_resid(3), TN_RES2 + 3)
                        if p == 6:
                            pe.wait_ge(turn_dve, TN_RES2 + 4)
                    elif p == 2:
                        pe.wait_ge(squared, i)
                        turn(halves(stage_q), TN_FFN2 + i - 1)
                    gemm(R, p, B_hi, B_lo, p, BK[3 if first else 0], p == 0, p == SPC - 1)

            ups2(R7, 0, first=True)

            def pass2(R, i, ready, steps=None):
                ups2(R, i)
                downs(R, SPC, D2_BANKS, [None, None, (up2_out, i + 1), (down2_out, 4 * i - 3)],
                      ready, steps)
                pe.wait_ge(down2_out, 4 * i - 1)

            def last_turn2(q):
                if q == 3:
                    pe.wait_ge(squared, FFN2)
                    turn(halves(stage_q), TN_FFN2 + FFN2 - 1)

            with pe.Fori(1, FFN2 - 1) as i:
                pass2(R7 + U2 + B7 * (i - 1), i, (turn_dve, TN_FFN2 + i))
            pass2(R_END - 2 - B7, FFN2 - 1, (turn_dve, TN_FFN2 + FFN2 - 1), last_turn2)
            ND2 = 4 * (FFN2 - 1)
            downs(R_END - 2, 0, D2_LAST, [None, None, (down2_out, ND2), (down2_out, ND2 + 1)],
                  (turn_dve, TN_FFN2 + FFN2), None, (A_hi, A_lo))

        @block.scalar
        def _(act):
            chain = Chain(act, act_self)

            def split(R, p):
                q = p + AHEAD
                act.wait_ge(landed[q % RING], 16 * (R + q // RING + 1))
                if not (isinstance(R, int) and R + q // RING == 0):
                    act.wait_ge(slot_done, RING * R + p)
                act.activation(w_hi[:, q % RING, :], raw[:, q % RING, :], ACT.Copy).then_inc(w_hi_ready, 1)

            def evacuate(dst, banks, scale, after, done, func=ACT.Copy, half=None, first=None):
                for t in range(TT):
                    if half and t == 0:
                        act.wait_ge(*half)
                    elif not half and t == 0 or half and t == 1:
                        act.wait_ge(slot_done, after)
                    m = act.activation(dst[:, t * CW:(t + 1) * CW], acc[:, banks[t], :], func, scale=scale[:, t:t + 1])
                    if first and t == 0:
                        m.then_inc(first, 1)
                m.then_inc(done, 1)

            def square(k, c):
                act.wait_ge(squares, NCH * k + c)
                for t in range(TT):
                    m = act.activation(junk[:, :], resid[:, t, c * CW:(c + 1) * CW], ACT.Square, scale=D ** -0.5,
                                       accum_out=ssq[:, t * NCH + c:t * NCH + c + 1])
                    if t < TT - 1:
                        chain.link(m)
                m.then_inc(squares, 1)

            def operand(n, hi, kt, g=None):
                act.wait_ge(turned, n + 1)
                if g is None:
                    m = act.activation(hi[:, kt:kt + JT, :].rearrange("p k t -> p (k t)"), turn_ps, ACT.Copy)
                else:
                    for j in range(JT):
                        m = act.activation(hi[:, kt + j, :], turn_ps[:, j * T:(j + 1) * T], ACT.Copy,
                                           scale=gain[:, g + kt + j:g + kt + j + 1])
                m.then_inc(turn_act, 1)

            def softmax(n, buf):
                act.wait_ge(masked, n + 1)
                for t in range(TT):
                    v = prob[:, buf, t * P:t * P + (t + 1) * P]
                    m = act.activation(v, v, ACT.Exp, scale=-1.0, bias=least[:, 2 * buf + t:2 * buf + t + 1],
                                       accum_out=psums[:, 2 * buf + t:2 * buf + t + 1])
                m.then_inc(exped, 1)

            def keep_probs(n):
                act.wait_ge(probs_turned, n + 1)
                act.wait_ge(mixed, n)
                act.activation(pT[:, :], acc[:, 7, 0:3 * P], ACT.Copy).then_inc(probs_kept, 1)

            def keep_mix(n, nth, dst):
                act.wait_ge(mixed, n + 1)
                act.activation(dst, acc[:, 5, 0:T].unsqueeze(1), ACT.Copy).then_inc(mixed_hi, 1)

            act.dma_start(ident, a["const"][:, C_ID:C_ID + P]).then_inc(ident_in, 16)
            act.dma_start(tabs[0:88, :, :], a["rows"].rearrange("(k r) c -> r k c", k=5)).then_inc(tab_in, 16)
            act.dma_start(fw_raw.rearrange("p (k n) -> p k n", k=KT),
                          a["w1"][:, 3 * D:3 * D + FOX_H].rearrange("(k p) n -> p k n", p=P)).then_inc(f_in, 16)
            act.dma_start(f_bias, a["b_f"].partition_broadcast(P)).then_inc(f_in, 16)
            act.dma_start(const[:, P:C_END], a["const"][:, P:C_END]).then_inc(const_in, 16)
            act.wait_ge(tabs_turned, 1)
            act.activation(gain[:, :], acc[:, 6, 0:G_END], ACT.Copy)
            act.activation(conv[:, 0:3, :], acc[:, 6, P:4 * P].rearrange("p (k c) -> p k c", k=3)[:, :, 0:88], ACT.Copy)
            chain.link(act.activation(conv[:, 3, :], acc[:, 7, 0:88], ACT.Copy))
            act.activation(fq_scale, gain[:, G_FQ:G_FQ + 1], ACT.Copy, scale=-float(P) ** -0.5).then_inc(tabs_kept, 1)
            split(0, -AHEAD)
            operand(TN_X, A_hi, 0, G_MIX)
            split(0, 1 - AHEAD)
            operand(TN_X + 1, A_hi, JT, G_MIX)
            split(0, 2 - AHEAD)

            def first_steps(p):
                if p in (1, 3):
                    c = 2 + p // 2
                    operand(TN_X + c, A_hi, c * JT, G_MIX)
                if p == 2:
                    act.wait_ge(filled, 5)
                    square(0, 0)
                if p == 4:
                    square(0, 1)
                if p == 5:
                    square(0, 2)
                    square(0, 3)
                if p == 6:
                    act.wait_ge(f_in, 32)
                    act.activation(fw_hi[:, :, :].rearrange("p k n -> p (k n)"), fw_raw, ACT.Copy).then_inc(f_hi, 1)
                    act.wait_ge(rstd_ready, 1)
                if p == 8:
                    act.wait_ge(lb_shift, 1)
                    act.activation(lb_tmp[:, 0:16], lb_tmp[:, 0:16], ACT.Exp).then_inc(lb_exp, 1)
                if p == 9:
                    act.wait_ge(f_turned, 1)
                    act.activation(f_lin, acc[0:FOX_H, 6, 0:T], ACT.Copy).then_inc(f_kept, 1)
                if p == 12:
                    act.wait_ge(f_z, 1)
                    chain.link(act.activation(f_abs, f_logit, ACT.Abs))
                    chain.link(act.activation(f_abs, f_abs, ACT.Exp, scale=-1.0))
                    act.activation(f_abs, f_abs, ACT.Ln, bias=1.0).then_inc(f_log, 1)
                if p == 7:
                    act.dma_start(until, a["until"]).then_inc(late_in, 16)
                if p == 14:
                    act.dma_start(unit(9), a["levels"]).then_inc(level_in, 16)
                    act.dma_start(hg_gain[:, :], a["hg_gain"].partition_broadcast(P)).then_inc(hg_gain_in, 16)

            def fox_step(kind, g, j):
                n = JT * g + j
                if kind == "turn_qk":
                    act.wait_ge(qk_turned, n + 1)
                    act.wait_ge(scored, n)
                    act.activation(qT, acc[:, 4, 0:T], ACT.Copy, scale=fq_scale)
                    act.activation(kT, acc[:, 4, T:2 * T], ACT.Copy, scale=gain[:, G_FK:G_FK + 1]).then_inc(qk_kept, 1)
                if kind == "score":
                    softmax(n, j % 2)
                if kind == "turn_p":
                    keep_probs(n)
                if kind == "mix":
                    keep_mix(n, n, B_hi[:, bass.ds(n, 1), :])

            def fox_pass(R, g, first=False):
                for p in range(3 * SPC):
                    split(R, p)
                    if first:
                        first_steps(p)
                    else:
                        for kind, j in fox_steps(p):
                            fox_step(kind, g - 1, j)
                    c, s = divmod(p, SPC)
                    if s == SPC - 1:
                        if not first:
                            act.wait_ge(*((mixed, JT * g) if c == 2 else (qk_turned, JT * g)))
                        evacuate((stage_q, stage_k, v_sb)[c], BK[c % 2], rstd, RING * R + p + 1, z1_out,
                                 half=(z1_half, 3 * g + c + 1), first=z1_first)

            fox_pass(R1, 0, first=True)
            fox_pass(R1 + F1, 1)
            with act.Fori(2, GROUPS) as g:
                fox_pass(R1 + F1 * g, g)
            for p in range(NCH * SPC):
                split(R2, p)
                for kind, j in fox_steps(p, last=True):
                    fox_step(kind, GROUPS - 1, j)
                for m in range(NCH - 1):
                    if p == OUT1_END[m] + 2:
                        operand(TN_RES1 + m, A_hi, m * JT, G_FFN)
                        square(1, m)

            def conv_tap(i, half, dst, n):
                act.wait_ge(turned, n + 1)
                for j in range(JT):
                    col = JT * i + j + half * (D_FF // P)
                    m = act.activation(dst[:, j * T:(j + 1) * T], turn_ps[:, j * T:(j + 1) * T], ACT.Identity,
                                       scale=conv[:, 2, bass.ds(col, 1)], bias=conv[:, 3, bass.ds(col, 1)])
                m.then_inc(turn_act, 1)

            def conv_value(i):
                conv_tap(i, 1, u_T, TN_FFN1 + 2 * i + 1)

            def gated_value(i, hi=C_hi):
                act.wait_ge(product, i + 1)
                act.activation(hi[:, 0:JT, :].rearrange("p k t -> p (k t)"), u_T, ACT.Copy).then_inc(gated_hi, 1)

            def ups1(R, i, first=False):
                for p in range(2 * SPC):
                    split(R, p)
                    if first and p == 2:
                        operand(TN_RES1 + 3, A_hi, 3 * JT, G_FFN)
                        square(1, 3)
                        act.wait_ge(rstd_ready, 2)
                    if not first and p == 1:
                        act.wait_ge(slot_done, RING * R)
                        conv_value(i - 1)
                    if not first and p == 2:
                        gated_value(i - 1)
                    if p == 10:
                        if not first:
                            act.wait_ge(product, i)
                        conv_tap(i, 0, g_T, TN_FFN1 + 2 * i)
                        act.wait_ge(turn_dve, TN_FFN1 + 2 * i + 1)
                        act.activation(s_T, g_T, ACT.Sigmoid).then_inc(gate_sig, 1)
                    if p % SPC == SPC - 1:
                        if not (first and p < SPC):
                            act.wait_ge(turned, TN_FFN1 + 2 * i + p // SPC)
                        evacuate(stage_q, BK[p // SPC], rstd, RING * R + p + 1, up1_out)

            ups1(R3, 0, first=True)
            with act.Fori(1, FFN1 - 1) as i:
                R = R3 + U1 + B3 * (i - 1)
                ups1(R, i)
                for q in range(2 * NCH):
                    split(R, 2 * SPC + q)
            ups1(R4 - 2 - B3, FFN1 - 1)
            for q in range(2 * NCH):
                split(R4 - 4, q)
                if q == 2:
                    act.wait_ge(gated, FFN1 - 1)
                    conv_value(FFN1 - 1)
                if q == 3:
                    gated_value(FFN1 - 1, B_hi)
            for q in range(2 * NCH):
                split(R4 - 2, q)
                if q >= 3 and q % 2 == 1:
                    m = (q - 3) // 2
                    operand(TN_DOWN1 + m, A_hi, m * JT, G_MIX2)
                    square(2, m)

            def keep_z2(c):
                after = RING * R4 + SPC * (c + 1)
                banks = BK[c % 2]
                if c < 8:
                    g, k = divmod(c, 4)
                    if k == 0 and g:
                        act.wait_ge(turned, TN_HG + 1)
                    if k == 1 and g:
                        act.wait_ge(turned, TN_HG + 2)
                    if k == 2 and g:
                        act.wait_ge(hg_mixed, 1)
                    if k == 3 and g:
                        act.wait_ge(hg_normed, 1)
                    evacuate((stage_q, stage_k, h_v, h_g)[k], banks, rstd, after, z2_out)
                    if k == 3:
                        act.wait_ge(turn_dve, TN_HG + 3 * g + 2)
                        act.wait_ge(z2_out, c + 1)
                        act.activation(unit(14), h_g, ACT.Sigmoid).then_inc(hg_sig, 1)
                elif 8 <= c < 11 or 14 <= c < 17:
                    g, k = divmod(c - 8, 6)
                    if k < 2:
                        act.wait_ge(*((qk_turned, FOX_H + 4) if g else (turned, TN_HG + 5)))
                        evacuate((stage_q, stage_k)[k], banks, rstd, after, z2_out)
                    else:
                        act.wait_ge(slot_done, after)
                        act.wait_ge(*((mixed, FOX_H + 8) if g else (zeroed, 1)))
                        for t in range(TT):
                            for u in range(2):
                                dst = v_pad[:, t, :, :].rearrange("p (j u) d -> p j u d", u=2)[:, :, u, u * AT_D:(u + 1) * AT_D]
                                src = acc[:, banks[t], :].rearrange("p (j u d) -> p j u d", u=2, d=AT_D)[:, :, u, :]
                                m = act.activation(dst, src, ACT.Copy, scale=rstd[:, t:t + 1])
                        m.then_inc(z2_out, 1)
                else:
                    if c == 11:
                        act.wait_ge(turned, TN_HG + 6)
                        act.wait_ge(hg_normed, 2)
                    if c == 21:
                        act.wait_ge(scored, FOX_H + AT_H)
                    evacuate(unit(GATE_U[c - 11 if c < 14 else c - 14]), banks, rstd, after, z2_out)

            def at_step(kind, g, j):
                n = FOX_H + 8 * g + j
                pair = FOX_H + 4 * g + j // 2
                if kind == "turn_qk":
                    act.wait_ge(qk_turned, pair + 1)
                    act.wait_ge(scored, n)
                    act.wait_ge(zeroed, 2)
                    act.activation(q2T, acc[:, 4, 0:T], ACT.Copy, scale=-float(AT_D) ** -0.5)
                    for u in range(2):
                        r = slice(u * AT_D, (u + 1) * AT_D)
                        m = act.activation(k2T[r, u, :], acc[r, 4, T:2 * T], ACT.Copy)
                    m.then_inc(qk_kept, 1)
                if kind == "score":
                    softmax(n, j % 2)
                if kind == "turn_p":
                    keep_probs(n)
                if kind == "mix" and j % 2 == 1:
                    keep_mix(n, pair, B_hi[:, pair - 8:pair - 7, :])

            for p in range(Z2 * SPC):
                split(R4, p)
                if p == 1:
                    operand(TN_DOWN1 + 3, A_hi, 3 * JT, G_MIX2)
                    square(2, 3)
                    act.wait_ge(rstd_ready, 3)
                step = hg_step(p)
                if step:
                    g, kind, k = step
                    if kind in ("turn_q", "turn_f"):
                        f = kind == "turn_f"
                        act.wait_ge(turned, TN_HG + 3 * g + f + 1)
                        act.wait_ge(turn_dve, TN_HG + 3 * g + f)
                        if g:
                            act.wait_ge(hg_gated, g)
                            act.wait_ge(hg_sums, g)
                        act.activation(unit(14), turn_ps, ACT.Sigmoid).then_inc(turn_act, 1)
                    if kind == "mix":
                        act.wait_ge(hg_mixed, g + 1)
                        act.wait_ge(hg_gated, g + 1)
                        act.activation(unit(14), pair3, ACT.Square, scale=P ** -0.5).then_inc(hg_square, 1)
                    if kind == "turn_y":
                        operand(TN_HG + 3 * g + 2, B_hi, g * JT)
                for kind, g, j in at_steps(p):
                    at_step(kind, g, j)
                if p % SPC == SPC - 1:
                    keep_z2(p // SPC)

            for p in range(NCH * SPC):
                split(R5, p)
                n, s = divmod(p, SPC)
                if p == 2 + SPC * n and n:
                    operand(TN_MERGE + n - 1, A_hi, (n - 1) * JT)
                if s == 0:
                    act.wait_ge(z2_out, Z2)
                    for k in range(2):
                        u = unit(GATE_U[n + NCH * k])
                        m = act.activation(u, u, ACT.Sigmoid)
                    m.then_inc(gate2_sig, 1)
            for p in range(NCH * SPC):
                split(R6, p)
                n, s = divmod(p, SPC)
                if p == 2:
                    operand(TN_MERGE + NCH - 1, A_hi, (NCH - 1) * JT)
                if p == 2 + SPC * n and n:
                    operand(TN_RES2 + n - 1, B_hi, (n - 1) * JT, G_MLP2)
                    square(3, n - 1)

            def ups2(R, i, first=False):
                for p in range(SPC):
                    split(R, p)
                    if first and p == 2:
                        operand(TN_RES2 + 3, B_hi, 3 * JT, G_MLP2)
                        square(3, 3)
                        act.wait_ge(rstd_ready, 4)
                    if not first and p == 2:
                        act.wait_ge(slot_done, RING * R)
                        operand(TN_FFN2 + i - 1, C_hi, 0)
                if not first:
                    act.wait_ge(turned, TN_FFN2 + i)
                evacuate(stage_q, BK[3 if first else 0], rstd, RING * R + SPC, up2_out, ACT.Relu)

            ups2(R7, 0, first=True)
            with act.Fori(1, FFN2 - 1) as i:
                R = R7 + U2 + B7 * (i - 1)
                ups2(R, i)
                for q in range(2 * NCH):
                    split(R, SPC + q)
            ups2(R_END - 2 - B7, FFN2 - 1)
            for q in range(2 * NCH):
                split(R_END - 4, q)
                if q == 3:
                    operand(TN_FFN2 + FFN2 - 1, A_hi, 0)
            for q in range(2 * NCH):
                if q + AHEAD < 2 * NCH:
                    split(R_END - 2, q)
                if q % 2 == 1:
                    act.wait_ge(down2_out, 4 * (FFN2 - 1) + q // 2 + 1)
                    square(4, q // 2)
            act.wait_ge(rstd_ready, 5)
            act.wait_ge(gained, NCH)
            for k in range(2):
                v = resid[:, 1, k * D // 2:(k + 1) * D // 2]
                act.activation(v, v, ACT.Copy, scale=rstd[:, 1:2]).then_inc(final_ready[1], 1)

        @block.vector
        def _(dve):
            chain = Chain(dve, dve_self)
            f32 = lambda ap: ap.bitcast(F32)

            def split(R, p):
                q = p + AHEAD
                dve.wait_ge(w_hi_ready, RING * R + q + 1)
                dve.tensor_tensor(w_lo[:, q % RING, :], raw[:, q % RING, :], f32(w_hi[:, q % RING, :]),
                                  ALU.subtract).then_inc(w_lo_ready, 1)

            def operand(n, hi, lo, kt, g=None):
                dve.wait_ge(turn_act, n + 1)
                if g is None:
                    m = dve.tensor_tensor(flat(lo[:, kt:kt + JT, :]), turn_ps, f32(flat(hi[:, kt:kt + JT, :])), ALU.subtract)
                else:
                    for j in range(JT):
                        m = dve.scalar_tensor_tensor(
                            out=lo[:, kt + j, :], in0=turn_ps[:, j * T:(j + 1) * T],
                            scalar=gain[:, g + kt + j:g + kt + j + 1], in1=f32(hi[:, kt + j, :]),
                            op0=ALU.mult, op1=ALU.subtract)
                m.then_inc(turn_dve, 1)

            def flat(v):
                return v.rearrange("p k t -> p (k t)")

            def sum_squares(k):
                dve.wait_ge(squares, NCH * (k + 1))
                dve.tensor_reduce(ssum, ssq.rearrange("p (t c) -> p t c", t=TT), AX_X, ALU.add).then_inc(sums, 1)

            def add_chunk(c, banks, after, done):
                dve.wait_ge(slot_done, after)
                v = resid[:, :, c * CW:(c + 1) * CW]
                dve.tensor_tensor(v, v, acc[:, banks[0]:banks[1] + 1, :], ALU.add).then_inc(done, 1)

            def heads_of(u):
                return u.rearrange("p (h d) -> p h d", d=P)

            def mask_scores(n, buf, mask):
                dve.wait_ge(scored, n + 1)
                dve.memset(wait_slot, 0.0)
                for t in range(TT):
                    v = slice(t * P, t * P + (t + 1) * P)
                    m = dve.tensor_tensor_reduce(
                        out=prob[:, buf, v], in0=acc[:, 6, v], in1=const[:, mask + (1 - t) * P:mask + 2 * P],
                        scale=1.0, scalar=3e38, op0=ALU.add, op1=ALU.min,
                        accum_out=least[:, 2 * buf + t:2 * buf + t + 1])
                m.then_inc(masked, 1)
                dve.wait_ge(exped, n + 1)
                chain.link(dve.reciprocal(precip[:, 2 * buf:2 * buf + 2], psums[:, 2 * buf:2 * buf + 2]))
                for t in range(TT):
                    v = prob[:, buf, t * P:t * P + (t + 1) * P]
                    m = dve.tensor_scalar(v, v, precip[:, 2 * buf + t:2 * buf + t + 1], None, ALU.mult)
                m.then_inc(probs, 1)

            def keep_mix(nth, hi, lo):
                dve.wait_ge(mixed_hi, nth + 1)
                dve.tensor_tensor(lo, acc[:, 5, 0:T].unsqueeze(1), f32(hi), ALU.subtract).then_inc(mixed_lo, 1)

            split(0, -AHEAD)
            operand(TN_X, A_hi, A_lo, 0, G_MIX)
            split(0, 1 - AHEAD)
            operand(TN_X + 1, A_hi, A_lo, JT, G_MIX)
            split(0, 2 - AHEAD)

            def first_steps(p):
                if p in (1, 3):
                    c = 2 + p // 2
                    operand(TN_X + c, A_hi, A_lo, c * JT, G_MIX)
                if p == 5:
                    sum_squares(0)
                if p == 6:
                    dve.wait_ge(const_in, 16)
                    dve.wait_ge(f_hi, 1)
                    dve.tensor_tensor(flat(fw_lo[:, :, :]), fw_raw, f32(flat(fw_hi[:, :, :])),
                                      ALU.subtract).then_inc(f_lo, 1)
                lb0, lb1 = gain[:, G_LB:G_LB + HG_H], gain[:, G_LB + HG_H:G_LB + 2 * HG_H]
                if p == 7:
                    chain.link(dve.tensor_tensor(lb_tmp[:, 16:24], lb0, lb1, ALU.max))
                    dve.tensor_tensor(lb_tmp[:, 0:8], lb0, lb_tmp[:, 16:24], ALU.subtract)
                    dve.tensor_tensor(lb_tmp[:, 8:16], lb1, lb_tmp[:, 16:24], ALU.subtract).then_inc(lb_shift, 1)
                if p == 9:
                    dve.wait_ge(lb_exp, 1)
                    chain.link(dve.tensor_tensor(lb_tmp[:, 16:24], lb_tmp[:, 0:8], lb_tmp[:, 8:16], ALU.add))
                    chain.link(dve.reciprocal(lb_tmp[:, 16:24], lb_tmp[:, 16:24]))
                    chain.link(dve.tensor_tensor(lbnd, lb_tmp[:, 0:8], lb_tmp[:, 16:24], ALU.mult))
                    chain.link(dve.tensor_scalar(one_lb, lbnd, -1.0, 1.0, ALU.mult, ALU.add))
                if p == 11:
                    dve.wait_ge(f_in, 32)
                    dve.wait_ge(f_turned, 2)
                    dve.wait_ge(rstd_ready, 1)
                    for t in range(TT):
                        v = slice(t * FOX_H, (t + 1) * FOX_H)
                        m = dve.scalar_tensor_tensor(out=f_logit[:, v], in0=acc[:, 6, T:T + TT * FOX_H][:, v],
                                                     scalar=rstd[:, t:t + 1], in1=f_bias, op0=ALU.mult, op1=ALU.add)
                    m.then_inc(f_z, 1)
                if p == 13:
                    dve.wait_ge(f_log, 1)
                    for k in range(4):
                        m = dve.scalar_tensor_tensor(out=logf[:, :, k * FOX_H:(k + 1) * FOX_H],
                                                     in0=f_logit.rearrange("p (t h) -> p t h", t=TT), scalar=0.0,
                                                     in1=f_abs.rearrange("p (t h) -> p t h", t=TT),
                                                     op0=ALU.min, op1=ALU.subtract)
                    m.then_inc(log_f, 1)
                if p == 2 * SPC:
                    dve.wait_ge(cum_turned, 1)
                    chain.link(dve.tensor_copy(cum_hi, acc[:, 7, 0:T]))
                    chain.link(dve.tensor_tensor(cum_lo, acc[:, 7, 0:T], f32(cum_hi), ALU.subtract))
                    for k, v in enumerate((cum_l, cum_r)):
                        c = C_AUG + 3 * k
                        chain.link(dve.tensor_scalar(cum_t, f32(cum_hi), const[:, c:c + 1], const[:, c + 2:c + 3],
                                                     ALU.mult, ALU.add))
                        m = dve.scalar_tensor_tensor(out=v, in0=f32(cum_lo), scalar=const[:, c + 1:c + 2], in1=cum_t,
                                                     op0=ALU.mult, op1=ALU.add)
                        if k == 0:
                            chain.link(m)
                    m.then_inc(cum_kept, 1)

            def head_squares(u, nth):
                dve.wait_ge(z1_out, nth)
                chain.link(dve.scalar_tensor_tensor(out=sq_sb, in0=u, scalar=1.0 / P, in1=u,
                                                    op0=ALU.mult, op1=ALU.mult))
                dve.tensor_reduce(head_ss, heads_of(sq_sb), AX_X, ALU.add).then_inc(head_sums, 1)

            def head_norm(u, nth):
                dve.wait_ge(head_rstd, nth)
                dve.tensor_tensor(heads_of(u), heads_of(u), head_rs.unsqueeze(2).to_broadcast([P, 2 * JT, P]),
                                  ALU.mult).then_inc(head_normed, 1)

            def fox_step(kind, g, j):
                n = JT * g + j
                if kind == "score":
                    mask_scores(n, j % 2, C_CAUSAL)
                if kind == "mix":
                    keep_mix(n, B_hi[:, bass.ds(n, 1), :], B_lo[:, bass.ds(n, 1), :])

            def fox_pass(R, g, first=False):
                for p in range(3 * SPC):
                    split(R, p)
                    if first:
                        first_steps(p)
                    else:
                        for kind, j in fox_steps(p):
                            fox_step(kind, g - 1, j)
                    if p == SPC + 3:
                        head_squares(stage_q, 3 * g + 1)
                    if p == SPC + 5:
                        head_norm(stage_q, 2 * g + 1)
                    if p == 2 * SPC:
                        head_squares(stage_k, 3 * g + 2)
                    if p == 2 * SPC + 2:
                        head_norm(stage_k, 2 * g + 2)

            fox_pass(R1, 0, first=True)
            fox_pass(R1 + F1, 1)
            with dve.Fori(2, GROUPS) as g:
                chain.enter(g, 2, JT + 2)
                fox_pass(R1 + F1 * g, g)
                chain.leave(GROUPS - 2)
            for p in range(NCH * SPC):
                split(R2, p)
                for kind, j in fox_steps(p, last=True):
                    fox_step(kind, GROUPS - 1, j)
                for m in range(NCH - 1):
                    if p == OUT1_END[m] + 2:
                        operand(TN_RES1 + m, A_hi, A_lo, m * JT, G_FFN)
                for m in range(NCH):
                    if p == OUT1_END[m] - 1:
                        add_chunk(m, BK[m % 2], RING * R2 + p + 1, res1_out)

            def conv_taps(i, half, dst, n):
                dve.wait_ge(turn_act, n + 1)
                for d in (1, 2):
                    for j in range(JT):
                        col = JT * i + j + half * (D_FF // P)
                        v = dst[:, j * T + d:(j + 1) * T]
                        m = dve.scalar_tensor_tensor(out=v, in0=turn_ps[:, j * T:(j + 1) * T - d],
                                                     scalar=conv[:, 2 - d, bass.ds(col, 1)], in1=v,
                                                     op0=ALU.mult, op1=ALU.add)
                    if d == 1:
                        chain.link(m)
                m.then_inc(turn_dve, 1)

            def value_steps(step, i, hi=C_hi, lo=C_lo):
                if step == 0:
                    conv_taps(i, 1, u_T, TN_FFN1 + 2 * i + 1)
                if step == 1:
                    gated_product(i)
                if step == 2:
                    dve.wait_ge(gated_hi, i + 1)
                    dve.tensor_tensor(flat(lo[:, 0:JT, :]), u_T, f32(flat(hi[:, 0:JT, :])), ALU.subtract).then_inc(gated, 1)

            def gated_product(i):
                dve.wait_ge(turn_dve, TN_FFN1 + 2 * i + 2)
                dve.tensor_tensor(u_T, u_T, g_T, ALU.mult).then_inc(product, 1)

            def ups1(R, i, first=False):
                for p in range(2 * SPC):
                    split(R, p)
                    if first and p == 2:
                        operand(TN_RES1 + 3, A_hi, A_lo, 3 * JT, G_FFN)
                        sum_squares(1)
                    if not first and 1 <= p <= 3:
                        value_steps(p - 1, i - 1)
                    if p == 10:
                        conv_taps(i, 0, g_T, TN_FFN1 + 2 * i)
                        dve.wait_ge(gate_sig, i + 1)
                        chain.link(dve.tensor_tensor(g_T, g_T, s_T, ALU.mult))

            def downs(R, p0, banks, done, ahead=True, steps=None):
                for q in range(2 * NCH):
                    if ahead or q + AHEAD < 2 * NCH:
                        split(R, p0 + q)
                    if steps:
                        steps(q)
                    if q % 2 == 1:
                        add_chunk(q // 2, banks[q // 2], RING * R + p0 + q + 1, done)

            ups1(R3, 0, first=True)
            with dve.Fori(1, FFN1 - 1) as i:
                chain.enter(i, 1, 3)
                R = R3 + U1 + B3 * (i - 1)
                ups1(R, i)
                downs(R, 2 * SPC, D1_BANKS, down1_out)
                chain.leave(FFN1 - 2)
            ups1(R4 - 2 - B3, FFN1 - 1)
            downs(R4 - 4, 0, D1_BANKS, down1_out, steps=lambda q: value_steps(q - 2, FFN1 - 1, B_hi, B_lo))

            def down1_steps(q):
                if q >= 3 and q % 2 == 1:
                    m = (q - 3) // 2
                    operand(TN_DOWN1 + m, A_hi, A_lo, m * JT, G_MIX2)

            downs(R4 - 2, 0, D1_BANKS, down1_out, steps=down1_steps)

            def blocks_of(u, h):
                return u.rearrange("p (b u h) -> p b u h", u=2, h=h)

            def make_level(g, k):
                h = 1 << (k - 1)
                z = blocks_of(Z[k % 2], h)
                q, kk, r, e = (blocks_of(u, h) for u in (h_q, h_k, run, rest))
                if k > 1:
                    dve.wait_ge(lv_done, (LEVELS + 1) * g + k - 1)
                dve.tensor_tensor(z[:, :, 0, :], kk[:, :, 0, :], e[:, :, 0, :], ALU.mult)
                dve.tensor_tensor(z[:, :, 1, :], q[:, :, 1, :], r[:, :, 1, :], ALU.mult).then_inc(lv_ready, 1)
                if k < LEVELS:
                    shape = [P, 1024 // (2 * h), h]
                    chain.link(dve.tensor_tensor(e[:, :, 0, :], e[:, :, 0, :], r[:, :, 1, h - 1:h].to_broadcast(shape),
                                                 ALU.mult))
                    chain.link(dve.tensor_tensor(r[:, :, 1, :], r[:, :, 1, :], r[:, :, 0, h - 1:h].to_broadcast(shape),
                                                 ALU.mult))

            def keep_level(g, k):
                n = (LEVELS + 1) * g + k
                dve.wait_ge(lv_done, n + 1)
                if k == 0 and g:
                    dve.wait_ge(hg_mixed, g)
                if n:
                    dve.wait_ge(lv_kept, n)
                o = turn_ps if k % 2 == 0 else pair3
                if k == LEVELS:
                    dve.tensor_copy(far, o[:, 0:CW]).then_inc(lv_kept, 1)
                else:
                    dve.copy_predicated(heads_of(near), levels[:, k, :].unsqueeze(1).to_broadcast([P, 2 * JT, P]),
                                        heads_of(o)).then_inc(lv_kept, 1)

            for p in range(Z2 * SPC):
                split(R4, p)
                if p == 1:
                    operand(TN_DOWN1 + 3, A_hi, A_lo, 3 * JT, G_MIX2)
                    sum_squares(2)
                    dve.wait_ge(hg_gain_in, 16)
                    dve.wait_ge(levels_made, 1)
                    dve.wait_ge(filled, 5)
                step = hg_step(p)
                if step:
                    g, kind, k = step
                    if kind == "turn_q":
                        dve.wait_ge(turn_act, TN_HG + 3 * g + 1)
                        if g:
                            dve.wait_ge(lv_done, LEVELS + 1)
                        dve.scalar_tensor_tensor(out=h_q, in0=turn_ps, scalar=float(P) ** -0.5, in1=unit(14),
                                                 op0=ALU.mult, op1=ALU.mult).then_inc(turn_dve, 1)
                    if kind == "turn_f":
                        dve.wait_ge(turn_act, TN_HG + 3 * g + 2)
                        for j in range(JT):
                            h = g * JT + j
                            v = slice(j * T, (j + 1) * T)
                            m = dve.tensor_scalar(run[:, v], unit(14)[:, v], one_lb[:, h:h + 1], lbnd[:, h:h + 1],
                                                  ALU.mult, ALU.add)
                        chain.link(m)
                        dve.tensor_scalar(h_k, run, -1.0, 1.0, ALU.mult, ALU.add).then_inc(turn_dve, 1)
                        dve.memset(rest, 1.0).then_inc(lv_ready, 1)
                        dve.wait_ge(lv_ready, (LEVELS + 1) * g + 1)
                        make_level(g, 1)
                    if kind == "level":
                        if 1 <= k < LEVELS:
                            make_level(g, k + 1)
                        keep_level(g, k)
                    if kind == "mix":
                        dve.wait_ge(hg_square, g + 1)
                        dve.tensor_reduce(head_ss, heads_of(unit(14)), AX_X, ALU.add).then_inc(hg_sums, 1)
                for g, b in enumerate(HG_AT):
                    if p == b + 32:
                        dve.wait_ge(hg_rstd, g + 1)
                        dve.wait_ge(hg_gated, g + 1)
                        chain.link(dve.tensor_tensor(heads_of(Z[0]), heads_of(pair3),
                                                     head_rs.unsqueeze(2).to_broadcast([P, 2 * JT, P]), ALU.mult))
                        dve.tensor_tensor(Z[0], Z[0], h_g, ALU.mult).then_inc(hg_normed, 1)
                    if p == b + 34:
                        operand(TN_HG + 3 * g + 2, B_hi, B_lo, g * JT)
                    if p == 4 * SPC * (g + 1):
                        dve.wait_ge(hg_sig, g + 1)
                        chain.link(dve.tensor_tensor(h_g, h_g, unit(14), ALU.mult))
                        dve.tensor_tensor(heads_of(h_g), heads_of(h_g),
                                          hg_gain[:, :].unsqueeze(1).to_broadcast([P, 2 * JT, P]),
                                          ALU.mult).then_inc(hg_gated, 1)
                for kind, g, j in at_steps(p):
                    if kind == "score":
                        mask_scores(FOX_H + 8 * g + j, j % 2, C_BAND)
                    if kind == "mix" and j % 2 == 1:
                        k = 8 + 4 * g + j // 2
                        keep_mix(8 + k, B_hi[:, k:k + 1, :], B_lo[:, k:k + 1, :])

            H = SPC // 2
            for p in range(NCH * SPC):
                split(R5, p)
                n, s = divmod(p, SPC)
                if p == 2 + SPC * n and n:
                    operand(TN_MERGE + n - 1, A_hi, A_lo, (n - 1) * JT)
                if s % H == H - 1:
                    k = s // H
                    dve.wait_ge(gate2_sig, n + 1)
                    dve.wait_ge(slot_done, RING * R5 + p + 1)
                    if k == 0 and n:
                        dve.wait_ge(turned, TN_MERGE + n)
                    g3 = unit(GATE_U[n + NCH * k]).rearrange("p (t c) -> p t c", t=TT)
                    dve.tensor_tensor((stage_q, stage_k)[k].rearrange("p (t c) -> p t c", t=TT), g3,
                                      acc[:, 2 * k:2 * k + 2, :], ALU.mult).then_inc(merge_read, 1)
                    if k == 1:
                        dve.wait_ge(merge_read, 2 * n + 2)
                        dve.tensor_tensor(stage_q, stage_q, stage_k, ALU.add).then_inc(merged_out, 1)
            for p in range(NCH * SPC):
                split(R6, p)
                n, s = divmod(p, SPC)
                if p == 2:
                    operand(TN_MERGE + NCH - 1, A_hi, A_lo, (NCH - 1) * JT)
                if p == 2 + SPC * n and n:
                    operand(TN_RES2 + n - 1, B_hi, B_lo, (n - 1) * JT, G_MLP2)
                if s == SPC - 1:
                    add_chunk(n, BK[n % 2], RING * R6 + p + 1, res2_out)

            def ups2(R, i, first=False):
                for p in range(SPC):
                    split(R, p)
                    if first and p == 2:
                        operand(TN_RES2 + 3, B_hi, B_lo, 3 * JT, G_MLP2)
                        sum_squares(3)
                    if not first and p == 2:
                        operand(TN_FFN2 + i - 1, C_hi, C_lo, 0)
                dve.wait_ge(up2_out, i + 1)
                dve.tensor_tensor(stage_q, stage_q, stage_q, ALU.mult).then_inc(squared, 1)

            ups2(R7, 0, first=True)
            with dve.Fori(1, FFN2 - 1) as i:
                R = R7 + U2 + B7 * (i - 1)
                ups2(R, i)
                downs(R, SPC, D2_BANKS, down2_out)
            ups2(R_END - 2 - B7, FFN2 - 1)
            downs(R_END - 4, 0, D2_BANKS, down2_out,
                  steps=lambda q: q == 3 and operand(TN_FFN2 + FFN2 - 1, A_hi, A_lo, 0))

            def gain_chunk(c):
                dve.wait_ge(squares, NCH * 4 + c + 1)
                v = slice(c * CW, (c + 1) * CW)
                dve.tensor_tensor(resid[:, :, v], resid[:, :, v], gain_out[:, v].unsqueeze(1).to_broadcast([P, TT, CW]),
                                  ALU.mult).then_inc(gained, 1)

            dve.wait_ge(gain_in, 16)
            downs(R_END - 2, 0, D2_LAST, down2_out, ahead=False,
                  steps=lambda q: q in (3, 5) and gain_chunk(q // 2 - 1))
            gain_chunk(NCH - 2)
            sum_squares(4)
            gain_chunk(NCH - 1)
            dve.wait_ge(rstd_ready, 5)
            dve.wait_ge(gained, NCH)
            for k in range(2):
                v = resid[:, 0, k * D // 2:(k + 1) * D // 2]
                dve.tensor_scalar(v, v, rstd[:, 0:1], None, ALU.mult).then_inc(final_ready[0], 1)

        @block.gpsimd
        def _(pool):
            chain = Chain(pool, pool_self)
            pool.memset(nothalf, -0.5).then_inc(filled, 1)
            pool.memset(eps, EPS).then_inc(filled, 1)
            pool.memset(logf, 0.0).then_inc(filled, 1)
            pool.memset(near, 0.0).then_inc(filled, 1)
            pool.memset(junk[:, :], 0.0).then_inc(filled, 1)
            pool.wait_ge(filled, 5)

            def inverse_root(out_, mean, width, done):
                chain.link(pool.tensor_tensor(mean_t[:, 0:width], mean, eps[:, 0:width], ALU.add))
                pool.tensor_tensor(out_, mean_t[:, 0:width], nothalf[:, 0:width], ALU.pow).then_inc(done, 1)

            def norm(k):
                pool.wait_ge(sums, k + 1)
                inverse_root(rstd, ssum, TT, rstd_ready)

            def head_norms(g):
                for k in range(2):
                    pool.wait_ge(head_sums, 2 * g + k + 1)
                    if not (isinstance(g, int) and g == 0 and k == 0):
                        pool.wait_ge(head_normed, 2 * g + k)
                    inverse_root(head_rs, head_ss, 2 * JT, head_rstd)

            def gate_rows(g, first=False):
                for j in range(JT):
                    n = JT * g + j
                    if not (first and j < 2):
                        pool.wait_ge(scored, n - 1)
                    pool.tensor_tensor(row_l[:, j % 2, :], cum_l,
                                       const[:, bass.ds(C_SEL + n, 1)].to_broadcast([P, T]),
                                       ALU.mult).then_inc(gates_row, 1)

            norm(0)
            head_norms(0)
            pool.wait_ge(level_in, 16)
            pool.tensor_copy(levels[:, :, :].rearrange("p l t -> p (l t)"), unit(9)).then_inc(levels_made, 1)
            pool.wait_ge(cum_kept, 1)
            gate_rows(0, first=True)
            head_norms(1)
            with pool.Fori(1, GROUPS - 1) as g:
                chain.enter(g, 1, 2)
                gate_rows(g)
                head_norms(g + 1)
                chain.leave(GROUPS - 2)
            gate_rows(GROUPS - 1)
            norm(1)
            pool.wait_ge(gated, FFN1)
            pool.memset(scratch[:, 2:4, :], 0.0).then_inc(zeroed, 1)
            norm(2)

            def load_bias(g):
                rel = a["rel"]
                src = bass.AP(tensor=rel.tensor, offset=rel[8 * g:8 * g + 1, REL - P + 1:REL - P + 2].offset,
                              ap=[[1, P], [2 * REL + 1, 8], [1, T]])
                pool.dma_start(bias_T, src).then_inc(bias_in[g], 16)

            for g in range(2):
                pool.wait_ge(hg_sums, g + 1)
                inverse_root(head_rs, head_ss, 2 * JT, hg_rstd)
                if g == 0:
                    pool.wait_ge(hg_normed, 1)
            pool.wait_ge(lv_ready, 2 * (LEVELS + 1))
            pool.wait_ge(lv_done, 2 * (LEVELS + 1))
            pool.memset(unit(6)[:, T:3 * T], 0.0).then_inc(zeroed, 1)
            load_bias(0)
            pool.wait_ge(scored, FOX_H + 8)
            load_bias(1)
            norm(3)
            pool.wait_ge(merged_out, NCH)
            pool.dma_start(gain_out, a["gain_out"].partition_broadcast(P)).then_inc(gain_in, 16)
            norm(4)


def kernel(**inputs):
    import concourse.bacc as bacc
    from concourse.bass_utils import run_bass_kernel_spmd

    def row_tiles(name, rows):
        return np.asarray(inputs[name]).reshape(rows, P)

    const, until, levels = constants()
    gains = np.concatenate([
        row_tiles("mix_norm", KT), row_tiles("ffn_norm", KT), row_tiles("norm_mix_w_2", KT),
        row_tiles("norm_mlp_w_2", KT), row_tiles("fox_q_gain", 1), row_tiles("fox_k_gain", 1),
        row_tiles("lb_logits_2", 2 * HG_H), np.zeros((88 - G_END, P), np.float32)])
    taps = np.asarray(inputs["ffn_conv_w"]).reshape(3 * 88, P)
    arrays = {
        "x": inputs["x"], "w1": inputs["fox_w_in"][0], "wo1": inputs["fox_w_out"][0],
        "up1": inputs["ffn_w_up"][0], "down1": inputs["ffn_w_down"][0], "w2": inputs["w_in_2"][0],
        "wa": inputs["w_branch_a_2"][0], "wb": inputs["w_branch_b_2"][0], "wo2": inputs["w_out_2"][0],
        "up2": inputs["w_up_2"][0], "down2": inputs["w_down_2"][0], "b_f": inputs["fox_b_f"][0],
        "rel": inputs["rel_bias_2"][0], "hg_gain": inputs["hg_norm_w_2"][0], "gain_out": inputs["norm_final_w_2"],
        "rows": np.concatenate([gains, taps, row_tiles("ffn_conv_b", 88)]),
        "const": const, "until": until, "levels": levels,
    }
    nc = bacc.Bacc("TRN2", target_bir_lowering=False, num_devices=1)
    fed, aps = {}, {}
    for name, v in arrays.items():
        v = np.ascontiguousarray(v)
        fed[f"in_{name}"] = v
        aps[name] = nc.dram_tensor(f"in_{name}", v.shape, mybir.dt.from_np(v.dtype), kind="ExternalInput").ap()
    out = nc.dram_tensor("out_h", (1, T, D), F32, kind="ExternalOutput").ap()
    build_program(nc, aps, out)
    r = run_bass_kernel_spmd(nc, [fed], core_ids=[0])
    return r.results[0]["out_h"]
```
